# Optimizing a Trainium2 kernel written in Bass

```python
import math
import jax, jax.numpy as jnp
from jax import lax
import numpy as np

D_MODEL = 1024
BATCH = 1
SEQ = 256
DEPTH = 2

A_HEADS = 6
A_HEAD_DIM = 64
A_CONFIGS = ((128, 1), (512, 4), (2048, 16))
B_HEADS = 4
B_QK_DIM = 64
B_V_DIM = 2 * B_QK_DIM
C_HEADS = 6
C_NOPE_DIM = 64
C_ROPE_DIM = 32
C_V_DIM = 64
C_Q_RANK = 256
C_KV_RANK = 128
ROPE_BASE = 10000.0
N_BUCKETS = 32
MAX_DISTANCE = 2048
BIAS_HEADS = A_HEADS + B_HEADS
PEER_HEADS = 8
PEER_KEYS = 128
PEER_EXPERTS = PEER_KEYS * PEER_KEYS
PEER_KEY_DIM = 128
PEER_TOPK = 16
PEER_CHUNK = 128
Q_BLOCK = 128
RMS_EPS = 1e-6
NEG_INF = -1e30

A_COLS = 3 * A_HEADS * A_HEAD_DIM
B_QK_COLS = B_HEADS * 2 * B_QK_DIM
B_V_COLS = B_HEADS * B_V_DIM
C_COLS = C_Q_RANK + C_KV_RANK + C_ROPE_DIM
GATE_COLS = 3 * D_MODEL
IN_COLS = A_COLS + 2 * B_QK_COLS + B_V_COLS + C_COLS + GATE_COLS
A_WIDTH = A_HEADS * A_HEAD_DIM
B_WIDTH = B_HEADS * B_V_DIM
C_WIDTH = C_HEADS * C_V_DIM

kernel_name = "hybrid_gated_dilated_diff_mla_peer"

def rmsnorm(x, g):
    xf = x.astype(jnp.float32)
    y = xf * lax.rsqrt(jnp.mean(xf * xf, axis=-1, keepdims=True) + RMS_EPS)
    return (y * g.astype(jnp.float32)).astype(x.dtype)

def t5_bucket(dist):
    n = jnp.maximum(dist, 0)
    max_exact = N_BUCKETS // 2
    nf = jnp.maximum(n, max_exact).astype(jnp.float32)
    large = max_exact + (jnp.log(nf / max_exact) / math.log(MAX_DISTANCE / max_exact)
                         * (N_BUCKETS - max_exact)).astype(jnp.int32)
    large = jnp.minimum(large, N_BUCKETS - 1)
    return jnp.where(n < max_exact, n, large)

def rope_tables(seq_len):
    half = C_ROPE_DIM // 2
    inv = ROPE_BASE ** (-jnp.arange(half, dtype=jnp.float32) / half)
    ang = jnp.arange(seq_len, dtype=jnp.float32)[:, None] * inv[None, :]
    return jnp.cos(ang), jnp.sin(ang)

def apply_rope(x, cos, sin):
    x1, x2 = jnp.split(x, 2, axis=-1)
    c = cos.astype(x.dtype)
    s = sin.astype(x.dtype)
    return jnp.concatenate([x1 * c - x2 * s, x1 * s + x2 * c], axis=-1)

def strided_window_attention(q, k, v, bias_table, window, dilation):
    bsz, seq, heads, dh = q.shape
    w = window // dilation
    span = w * dilation
    sp = -(-seq // span) * span
    pad = sp - seq
    nb = sp // span

    def to_blocks(t):
        t = jnp.pad(t, ((0, 0), (0, pad), (0, 0), (0, 0)))
        t = t.reshape(bsz, sp // dilation, dilation, heads, dh)
        t = t.transpose(0, 2, 1, 3, 4)
        return t.reshape(bsz, dilation, nb, w, heads, dh)

    def with_prev(t):
        prev = jnp.pad(t[:, :, :-1], ((0, 0), (0, 0), (1, 0), (0, 0), (0, 0), (0, 0)))
        return jnp.concatenate([prev, t], axis=3)

    qb = to_blocks(q)
    kk = with_prev(to_blocks(k))
    vv = with_prev(to_blocks(v))
    logits = jnp.einsum('brnqhd,brnkhd->brnhqk', qb, kk).astype(jnp.float32) / math.sqrt(dh)
    qi = jnp.arange(w)[:, None]
    ki = jnp.arange(2 * w)[None, :]
    rel = w + qi - ki
    band = (rel >= 0) & (rel <= w)
    bias = bias_table[t5_bucket(rel * dilation)].astype(jnp.float32)
    logits = logits + bias.transpose(2, 0, 1)
    first = (jnp.arange(nb)[:, None, None] == 0) & (ki[None] < w)
    valid = band[None] & ~first
    logits = jnp.where(valid[None, None, :, None], logits, NEG_INF)
    lse = jax.nn.logsumexp(logits, axis=-1)
    p = jnp.exp(logits - lse[..., None]).astype(v.dtype)
    out = jnp.einsum('brnhqk,brnkhd->brnqhd', p, vv)
    out = out.reshape(bsz, dilation, sp // dilation, heads, dh).transpose(0, 2, 1, 3, 4)
    out = out.reshape(bsz, sp, heads, dh)[:, :seq]
    lse = lse.transpose(0, 1, 2, 4, 3).reshape(bsz, dilation, sp // dilation, heads)
    lse = lse.transpose(0, 2, 1, 3).reshape(bsz, sp, heads)[:, :seq]
    return out, lse

def dilated_attention(q, k, v, bias_table):
    outs, lses = [], []
    for window, dilation in A_CONFIGS:
        o, l = strided_window_attention(q, k, v, bias_table, window, dilation)
        outs.append(o)
        lses.append(l)
    wts = jax.nn.softmax(jnp.stack(lses, 0), axis=0)
    return jnp.einsum('gbsh,gbshd->bshd', wts.astype(q.dtype), jnp.stack(outs, 0))

def to_qblocks(t):
    bsz, heads, seq, dd = t.shape
    return t.reshape(bsz, heads, seq // Q_BLOCK, Q_BLOCK, dd).transpose(2, 0, 1, 3, 4)

def from_qblocks(out):
    nb, bsz, heads, qb, dd = out.shape
    return out.transpose(1, 0, 3, 2, 4).reshape(bsz, nb * qb, heads, dd)

def diff_attention(q1, q2, k1, k2, v, bias_table, lam, lam_init, subln_g):
    bsz, heads, seq, d = q1.shape
    nb = seq // Q_BLOCK
    scale = 1.0 / math.sqrt(d)
    kpos = jnp.arange(seq)

    def body(args):
        i, qa, qb = args
        qpos = i * Q_BLOCK + jnp.arange(Q_BLOCK)
        dist = qpos[:, None] - kpos[None, :]
        causal = dist >= 0
        bias = bias_table[t5_bucket(dist)].astype(jnp.float32).transpose(2, 0, 1)

        def probs(qx, kx):
            s = jnp.einsum('bhqd,bhkd->bhqk', qx, kx).astype(jnp.float32) * scale + bias
            return jax.nn.softmax(jnp.where(causal, s, NEG_INF), axis=-1)

        a = probs(qa, k1) - lam * probs(qb, k2)
        return jnp.einsum('bhqk,bhkd->bhqd', a.astype(v.dtype), v)

    out = lax.map(body, (jnp.arange(nb), to_qblocks(q1), to_qblocks(q2)))
    out = from_qblocks(out)
    out = rmsnorm(out, subln_g) * (1.0 - lam_init)
    return out.reshape(bsz, seq, heads * 2 * d)

def mla_attention(q_nope, q_rope, k_nope, k_rope, v):
    bsz, heads, seq, _ = q_nope.shape
    nb = seq // Q_BLOCK
    scale = 1.0 / math.sqrt(C_NOPE_DIM + C_ROPE_DIM)
    kpos = jnp.arange(seq)

    def body(args):
        i, qn, qr = args
        qpos = i * Q_BLOCK + jnp.arange(Q_BLOCK)
        causal = (qpos[:, None] - kpos[None, :]) >= 0
        s = (jnp.einsum('bhqd,bhkd->bhqk', qn, k_nope)
             + jnp.einsum('bhqd,bkd->bhqk', qr, k_rope)).astype(jnp.float32) * scale
        p = jax.nn.softmax(jnp.where(causal, s, NEG_INF), axis=-1)
        return jnp.einsum('bhqk,bhkd->bhqd', p.astype(v.dtype), v)

    out = lax.map(body, (jnp.arange(nb), to_qblocks(q_nope), to_qblocks(q_rope)))
    return from_qblocks(out).reshape(bsz, seq, heads * C_V_DIM)

def peer_ffn(h, w_q, sub_keys, u, v_e):
    bsz, seq, d = h.shape
    q = (h @ w_q).reshape(bsz, seq, PEER_HEADS, 2, PEER_KEY_DIM // 2)
    scores = jnp.einsum('bshpd,hpkd->bshpk', q, sub_keys).astype(jnp.float32)
    top_s, top_i = lax.top_k(scores, PEER_TOPK)
    cand = top_s[..., 0, :, None] + top_s[..., 1, None, :]
    best_s, best_c = lax.top_k(cand.reshape(bsz, seq, PEER_HEADS, PEER_TOPK * PEER_TOPK), PEER_TOPK)
    i1 = jnp.take_along_axis(top_i[..., 0, :], best_c // PEER_TOPK, axis=-1)
    i2 = jnp.take_along_axis(top_i[..., 1, :], best_c % PEER_TOPK, axis=-1)
    idx = i1 * PEER_KEYS + i2
    gate = jax.nn.softmax(best_s, axis=-1).astype(h.dtype)
    n_chunks = (bsz * seq) // PEER_CHUNK
    idx = idx.reshape(n_chunks, PEER_CHUNK, PEER_HEADS * PEER_TOPK)
    gate = gate.reshape(n_chunks, PEER_CHUNK, PEER_HEADS * PEER_TOPK)
    hc = h.reshape(n_chunks, PEER_CHUNK, d)

    def body(args):
        ic, gc, xc = args
        act = jax.nn.gelu(jnp.einsum('tkd,td->tk', u[ic], xc), approximate=False)
        return jnp.einsum('tk,tkd->td', gc * act, v_e[ic])

    out = lax.map(body, (idx, gate, hc))
    return out.reshape(bsz, seq, d)

def split_in_proj(proj):
    sizes = [A_COLS, B_QK_COLS, B_QK_COLS, B_V_COLS, C_Q_RANK, C_KV_RANK, C_ROPE_DIM]
    bounds, acc = [], 0
    for s in sizes:
        acc += s
        bounds.append(acc)
    return jnp.split(proj, bounds, axis=-1)

def setup_inputs(seed: int = 0) -> dict:
    key = jax.random.key(seed)
    ks = jax.random.split(key, 24)
    f32 = jnp.float32

    def nrm(k, shape, scale):
        return jax.random.normal(k, shape, f32) * scale

    def gain(k, shape):
        return 1.0 + 0.02 * jax.random.normal(k, shape, f32)

    L, D = DEPTH, D_MODEL
    return {
        "x": nrm(ks[0], (BATCH, SEQ, D), 1.0),
        "rel_bias": nrm(ks[1], (N_BUCKETS, BIAS_HEADS), 0.5),
        "w_in": nrm(ks[2], (L, D, IN_COLS), D ** -0.5),
        "g_mix": gain(ks[3], (L, D)),
        "w_uq": nrm(ks[4], (L, C_Q_RANK, C_HEADS * (C_NOPE_DIM + C_ROPE_DIM)), C_Q_RANK ** -0.5),
        "g_cq": gain(ks[5], (L, C_Q_RANK)),
        "w_ukv": nrm(ks[6], (L, C_KV_RANK, C_HEADS * (C_NOPE_DIM + C_V_DIM)), C_KV_RANK ** -0.5),
        "g_ckv": gain(ks[7], (L, C_KV_RANK)),
        "lam_q1": nrm(ks[8], (L, B_QK_DIM), 0.1),
        "lam_k1": nrm(ks[9], (L, B_QK_DIM), 0.1),
        "lam_q2": nrm(ks[10], (L, B_QK_DIM), 0.1),
        "lam_k2": nrm(ks[11], (L, B_QK_DIM), 0.1),
        "g_subln": gain(ks[12], (L, B_V_DIM)),
        "w_branch_a": nrm(ks[13], (L, A_WIDTH, D), A_WIDTH ** -0.5),
        "w_branch_b": nrm(ks[14], (L, B_WIDTH, D), B_WIDTH ** -0.5),
        "w_branch_c": nrm(ks[15], (L, C_WIDTH, D), C_WIDTH ** -0.5),
        "w_out": nrm(ks[16], (L, D, D), D ** -0.5),
        "g_ffn": gain(ks[17], (L, D)),
        "w_peer_q": nrm(ks[18], (L, D, PEER_HEADS * PEER_KEY_DIM), D ** -0.5),
        "peer_sub_keys": nrm(ks[19], (L, PEER_HEADS, 2, PEER_KEYS, PEER_KEY_DIM // 2), (PEER_KEY_DIM // 2) ** -0.5),
        "peer_u": nrm(ks[20], (L, PEER_EXPERTS, D), D ** -0.5),
        "peer_v": nrm(ks[21], (L, PEER_EXPERTS, D), (PEER_HEADS * PEER_TOPK) ** -0.5),
        "g_final": gain(ks[22], (D,)),
    }

def reference(x, rel_bias, w_in, g_mix, w_uq, g_cq, w_ukv, g_ckv, lam_q1, lam_k1, lam_q2, lam_k2,
              g_subln, w_branch_a, w_branch_b, w_branch_c, w_out, g_ffn, w_peer_q, peer_sub_keys,
              peer_u, peer_v, g_final):
    bsz, seq, d = x.shape
    cos, sin = rope_tables(seq)
    bias_a = rel_bias[:, :A_HEADS]
    bias_b = rel_bias[:, A_HEADS:]
    for l in range(DEPTH):
        h = rmsnorm(x, g_mix[l])
        proj = h @ w_in[l]
        a_qkv, b_q, b_k, b_v, c_q, c_kv, c_kr, gates = split_in_proj(proj)

        a = a_qkv.reshape(bsz, seq, 3, A_HEADS, A_HEAD_DIM)
        y_a = dilated_attention(a[:, :, 0], a[:, :, 1], a[:, :, 2], bias_a).reshape(bsz, seq, A_WIDTH)

        bq = b_q.reshape(bsz, seq, B_HEADS, 2, B_QK_DIM).transpose(3, 0, 2, 1, 4)
        bk = b_k.reshape(bsz, seq, B_HEADS, 2, B_QK_DIM).transpose(3, 0, 2, 1, 4)
        bv = b_v.reshape(bsz, seq, B_HEADS, B_V_DIM).transpose(0, 2, 1, 3)
        lam_init = 0.8 - 0.6 * math.exp(-0.3 * l)
        lam = (jnp.exp(jnp.sum(lam_q1[l].astype(jnp.float32) * lam_k1[l].astype(jnp.float32)))
               - jnp.exp(jnp.sum(lam_q2[l].astype(jnp.float32) * lam_k2[l].astype(jnp.float32)))
               + lam_init)
        y_b = diff_attention(bq[0], bq[1], bk[0], bk[1], bv, bias_b, lam, lam_init, g_subln[l])

        cq = (rmsnorm(c_q, g_cq[l]) @ w_uq[l]).reshape(bsz, seq, C_HEADS, C_NOPE_DIM + C_ROPE_DIM)
        q_nope, q_rope = cq[..., :C_NOPE_DIM], cq[..., C_NOPE_DIM:]
        q_rope = apply_rope(q_rope, cos[:, None, :], sin[:, None, :])
        ckv = (rmsnorm(c_kv, g_ckv[l]) @ w_ukv[l]).reshape(bsz, seq, C_HEADS, C_NOPE_DIM + C_V_DIM)
        k_nope, v_c = ckv[..., :C_NOPE_DIM], ckv[..., C_NOPE_DIM:]
        k_rope = apply_rope(c_kr, cos, sin)
        y_c = mla_attention(q_nope.transpose(0, 2, 1, 3), q_rope.transpose(0, 2, 1, 3),
                            k_nope.transpose(0, 2, 1, 3), k_rope, v_c.transpose(0, 2, 1, 3))

        g = jax.nn.sigmoid(gates.reshape(bsz, seq, 3, d))
        mix = (g[:, :, 0] * (y_a @ w_branch_a[l])
               + g[:, :, 1] * (y_b @ w_branch_b[l])
               + g[:, :, 2] * (y_c @ w_branch_c[l]))
        x = x + mix @ w_out[l]

        h2 = rmsnorm(x, g_ffn[l])
        x = x + peer_ffn(h2, w_peer_q[l], peer_sub_keys[l], peer_u[l], peer_v[l])
    return rmsnorm(x, g_final)


_drawn_inputs = setup_inputs


def setup_inputs(seed=0):
    import zlib

    import numpy as np

    out = dict(_drawn_inputs(seed))
    spreads = {}
    factors = {'g_mix': 2.724,
     'g_cq': 8.0,
     'g_ckv': 8.0,
     'lam_q1': 3.042,
     'lam_k2': 2.762,
     'g_subln': 4.77,
     'g_ffn': 6.393,
     'g_final': 2.825}
    for name, (base, spread) in spreads.items():
        noise = np.random.default_rng([zlib.crc32(name.encode()), seed]).standard_normal(out[name].shape)
        drawn = base * np.exp(spread * noise) if base else spread * noise
        out[name] = __import__('jax').numpy.asarray(drawn.astype(out[name].dtype))
    for name, factor in factors.items():
        out[name] = (out[name] * factor).astype(out[name].dtype)
    return out
```

```python
import math
from contextlib import ExitStack

import concourse.bass as bass
from concourse import mybir

F32 = mybir.dt.float32
U32 = mybir.dt.uint32
ALU = mybir.AluOpType
ACT = mybir.ActivationFunctionType
AX = mybir.AxisListType

P = 128
D = 1024
SEQ = 256
DEPTH = 2
TILES = SEQ // P
STAGES = DEPTH * TILES
KC = D // P
A_HEADS, B_HEADS, C_HEADS, HD = 6, 4, 6, 64
A_CONFIGS = ((128, 1), (512, 4), (2048, 16))
ROPE = 32
C_QK = HD + ROPE
Q_RANK, KV_RANK = 256, 128
BUCKETS, MAX_DISTANCE = 32, 2048
BIAS_HEADS = A_HEADS + B_HEADS
EPS = 1e-6
NEG = -1e30
DISTS = 3 * P
HEADS, KEYS, TOPK = 8, 128, 16
EXPERTS = KEYS * KEYS
PICKS = HEADS * TOPK

COL_AQ, COL_AK, COL_AV = 0, 384, 768
COL_BQ, COL_BK, COL_BV = 1152, 1664, 2176
COL_C, C_WIDTH = 2688, Q_RANK + KV_RANK + ROPE
COL_GATE = 3104
GATE_CHUNKS = 6
BANK = 512

(HT0, HT1, PC, AQ, AK, AV, CT, CQ0, CQ1, CKV0, CKV1, BQ, BK, BV, CQT0, CQT1, CKT0, CKT1,
 GATE0) = range(19)
YT0 = GATE0 + GATE_CHUNKS
BR0 = YT0 + 3
MT0 = BR0 + 6
WO0 = MT0 + 2
H2T0 = WO0 + 2
PQ0 = H2T0 + 2
USES = PQ0 + 2

W_CHUNKS = ([("c", PC), ("aq", AQ), ("ak", AK), ("av", AV), ("bq", BQ), ("bk", BK), ("bv", BV)]
            + [(("gate", g), GATE0 + g) for g in range(GATE_CHUNKS)]
            + [("wa", BR0 + 3), ("wb", BR0 + 4), ("wc", BR0 + 5), (("wo", 0), WO0), (("wo", 1), WO0 + 1),
               (("pq", 0), PQ0), (("pq", 1), PQ0 + 1)])
W_AT = {name: i for i, (name, _) in enumerate(W_CHUNKS)}
NW = len(W_CHUNKS)
W_SLOTS = 3
W_WORDS = 4096

GROUPS = 10
RING = 8


def kind_of(g):
    return ("A", g) if g < 3 else ("B", g - 3) if g < 7 else ("C", g - 7)


class Mark:

    def __init__(self, sem, per_stage):
        self.sem, self.per_stage = sem, per_stage

    def at(self, s, i=0):
        return s * self.per_stage + i + 1


def trunk(nc, x, rel_bias, w_in, g_mix, w_uq, g_cq, w_ukv, g_ckv, lam_vecs, g_subln, w_a, w_b, w_c, w_out, g_ffn,
          w_pq, keysT, peer_u, peer_v, g_final, ident_in, onehot_in, maskrow_in, count_in, rope_in, iota_in, out):
    table_dram = nc.dram_tensor("distance_bias", [BIAS_HEADS + 1, P, DISTS], F32, kind="Internal").ap()
    with ExitStack() as ctx:
        def sb(name, shape, dt=F32):
            return ctx.enter_context(nc.sbuf_tensor(name, shape, dt))

        def sem(name):
            return ctx.enter_context(nc.semaphore(name))

        def mark(name, per_stage):
            return Mark(sem(name), per_stage)

        rows = sb("rows", [P, RING, D])
        weights = sb("weights", [P, W_SLOTS, W_WORDS])
        ident = sb("ident", [P, P])
        bias = sb("bias", [P, BIAS_HEADS + 1, SEQ])
        count = sb("count", [P, SEQ])
        rope = sb("rope", [P, TILES, 2, 7 * 16])
        iota = sb("iota", [P, TOPK])
        headrow = sb("headrow", [BUCKETS + 2, BIAS_HEADS + 1])
        eps = sb("eps", [P, 1])
        xs = sb("xs", [P, TILES, D])
        gmix = sb("gmix", [P, D])
        gffn = sb("gffn", [P, D])
        gcq = sb("gcq", [P, Q_RANK])
        gckv = sb("gckv", [P, KV_RANK])
        gsub = sb("gsub", [P, P])
        lams = sb("lams", [P, DEPTH, 2])
        neglam = sb("neglam", [P, DEPTH])
        wuq = sb("wuq", [P, 2, C_HEADS * C_QK])
        wukv = sb("wukv", [P, C_HEADS * P])
        keys = sb("keys", [P, HEADS, KEYS])
        hrow = sb("hrow", [P, D])
        hT = sb("hT", [P, KC, P])
        h2row = sb("h2row", [P, D])
        stat = sb("stat", [P, 16])
        qTA = sb("qTA", [P, 3, P])
        kTA = sb("kTA", [P, 3, SEQ])
        vA = sb("vA", [P, TILES, A_HEADS * HD])
        qTB = sb("qTB", [P, B_HEADS, P])
        kTB = sb("kTB", [P, B_HEADS, SEQ])
        vB = sb("vB", [P, TILES, B_HEADS * 2 * HD])
        krot = sb("krot", [P, ROPE])
        qTC = sb("qTC", [C_QK, C_HEADS, P])
        kTC = sb("kTC", [C_QK, C_HEADS, SEQ])
        vC = sb("vC", [P, TILES, C_HEADS * HD])
        logits = sb("logits", [P, 2, 2, SEQ])
        negmax = sb("negmax", [P, 2, 2])
        probs = sb("probs", [P, 2, 2, SEQ])
        denom = sb("denom", [P, 2, 2])
        recip = sb("recip", [P, 2, 2])
        lamr = sb("lamr", [P, 1])
        probsT = sb("probsT", [P, 2, BANK])
        mixers = sb("mixers", [P, 2 * 10 * P])
        gates = sb("gates", [P, GATE_CHUNKS * BANK])
        tops = sb("tops", [P, HEADS * 2, TOPK])
        topi = sb("topi", [P, HEADS * 2, TOPK], U32)
        best = sb("best", [P, HEADS, TOPK])
        bestpos = sb("bestpos", [P, HEADS, TOPK], U32)
        gsum = sb("gsum", [P, 2, HEADS])
        pickw = sb("pickw", [P, 2, PICKS])
        index = sb("index", [P, 2, PICKS], U32)
        indexh = sb("indexh", [P, 2, TOPK], U32)
        acts = sb("acts", [P, PICKS])
        coef = sb("coef", [P, PICKS])

        y = mixers[:, 0:10 * P]
        yT = mixers[:, 10 * P:20 * P].rearrange("p (b t) -> p b t", b=10)
        scores = mixers[:, 0:HEADS * 2 * KEYS].rearrange("p (j k) -> p j k", k=KEYS)
        onehot = mixers[0:BUCKETS + 2, 0:BANK]
        table = mixers[0:BIAS_HEADS + 1, BANK:2 * BANK]
        lamv = mixers[:, 2 * BANK:3 * BANK].rearrange("p (l v d) -> p l v d", l=DEPTH, v=4)
        pqT = probs[:, :, :, :].rearrange("p a b c -> p (a b c)").rearrange("p (h t) -> p h t", h=HEADS)

        def before_gates(at, n):
            return gates[:, at:at + n], at + n

        crow, at = before_gates(0, C_WIDTH)
        cnorm, at = before_gates(at, Q_RANK + KV_RANK)
        cT, at = before_gates(at, 3 * P)
        qrow, at = before_gates(at, C_HEADS * C_QK)
        krow, at = before_gates(at, C_HEADS * C_QK)
        rot, at = before_gates(at, 4 * 7 * 16)
        assert at <= GATE_CHUNKS * BANK
        cT = cT.rearrange("p (c t) -> p c t", c=3)
        qrow, krow = (z.rearrange("p (h c) -> p h c", h=C_HEADS) for z in (qrow, krow))
        rot = rot.rearrange("p (j n) -> p j n", j=4)
        cand = gates[:, 0:PICKS * TOPK]
        at = PICKS * TOPK
        topf, at = gates[:, at:at + HEADS * 2 * TOPK].rearrange("p (j k) -> p j k", k=TOPK), at + HEADS * 2 * TOPK
        pos, at = gates[:, at:at + 2 * PICKS].bitcast(U32).rearrange("p (j k) -> p j k", j=2), at + 2 * PICKS
        posf, at = gates[:, at:at + 2 * PICKS].rearrange("p (j k) -> p j k", j=2), at + 2 * PICKS
        part, at = gates[:, at:at + 2 * PICKS].rearrange("p (j k) -> p j k", j=2), at + 2 * PICKS
        mix = hrow
        tmp = logits[:, 0, :, :].rearrange("p a b -> p (a b)")

        def ps(name, words):
            return ctx.enter_context(nc.psum_tensor(name, [P, words], F32))

        proj = [ps(f"proj{i}", BANK) for i in range(2)]
        sc = [ps(f"sc{i}", 2 * BANK) for i in range(2)]
        psT = ps("psT", BANK)
        psO = ps("psO", BANK)

        x_in, ident_sem, consts_in, table_out, bias_in = (sem(n) for n in (
            "x_in", "ident_in", "consts_in", "table_out", "bias_in"))
        lam_in, head_in = sem("lam_in"), sem("head_in")
        mix_params = sem("mix_params")
        ffn_params = sem("ffn_params")
        final_params = sem("final_params")
        w_in_sem = [sem(f"w_in{i}") for i in range(W_SLOTS)]
        row_in = [sem(f"row_in{i}") for i in range(RING)]
        headrow_zero, table_ps, table_sb, eps_set = (sem(n) for n in (
            "headrow_zero", "table_ps", "table_sb", "eps_set"))
        lam_sums, lam_exps = sem("lam_sums"), sem("lam_exps")
        proj_ready = mark("proj_ready", USES)
        proj_free = [sem("proj_free0"), sem("proj_free1")]
        h_ready = mark("h_ready", 1)
        mean_ready = mark("mean_ready", 4)
        root_ready = mark("root_ready", 4)
        cnorm_ready = mark("cnorm_ready", 1)
        qrope_ready = mark("qrope_ready", 1)
        krope_ready = mark("krope_ready", 1)
        s_ready = mark("s_ready", GROUPS)
        neg_ready = mark("neg_ready", GROUPS)
        e_ready = mark("e_ready", GROUPS)
        p_ready = mark("p_ready", GROUPS)
        pT_ready = mark("pT_ready", GROUPS)
        pTs_ready = mark("pTs_ready", GROUPS)
        o_ready = mark("o_ready", GROUPS)
        o_used = mark("o_used", GROUPS)
        y_ready = mark("y_ready", 1)
        sig_ready = mark("sig_ready", 1)
        mix_ready = mark("mix_ready", 2)
        h2_ready = mark("h2_ready", 1)
        route_ready = mark("route_ready", 2)
        best_ready = mark("best_ready", 1)
        bexp_ready = mark("bexp_ready", 1)
        index_ready = mark("index_ready", 1)
        index_copied = sem("index_copied")

        rows_used = sem("rows_used")
        pool_steps = sem("pool_steps")
        gelu_ready = mark("gelu_ready", 1)
        coef_ready = mark("coef_ready", 1)
        fin_mean, fin_root, fin_row = sem("fin_mean"), sem("fin_root"), sem("fin_row")
        out_written = sem("out_written")
        dve_done = sem("dve_done")
        act_done = sem("act_done")

        def bank_of(s, use):
            return (s * USES + use) % 2

        def freed(s, use):
            return (s * USES + use) // 2 + 1

        def w_view(s, name, kc):
            n = s * NW + W_AT[name]
            return weights[:, n % W_SLOTS, :].rearrange("p (c n) -> p c n", c=kc)

        def row_step(s, phase, k):
            return (s * 2 + phase) * PICKS + k

        block = ctx.enter_context(nc.Block())

        @block.sync
        def _(sp):
            def bcast(vec):
                return vec.partition_broadcast(P)

            def load_mix_params(l):
                for dst, src in ((gmix[:, :], bcast(g_mix[l])), (gcq[:, :], bcast(g_cq[l])),
                                 (gckv[:, :], bcast(g_ckv[l])), (gsub[:, :], bcast(g_subln[l])),
                                 (wuq[:, :, :], w_uq[l].rearrange("(c p) n -> p c n", p=P)), (wukv[:, :], w_ukv[l])):
                    sp.dma_start(dst, src).then_inc(mix_params, 16)

            def load_ffn_params(l):
                sp.dma_start(gffn[:, :], bcast(g_ffn[l])).then_inc(ffn_params, 16)
                sp.dma_start(keys[:, :, :], keysT[l].rearrange("p (h k) -> p h k", h=HEADS)).then_inc(ffn_params, 16)

            def source(l, name):
                cols = {"c": (COL_C, C_WIDTH), "aq": (COL_AQ, 384), "ak": (COL_AK, 384), "av": (COL_AV, 384),
                        "bq": (COL_BQ, 512), "bk": (COL_BK, 512), "bv": (COL_BV, 512)}
                if name in ("wa", "wb", "wc"):
                    w = {"wa": w_a, "wb": w_b, "wc": w_c}[name]
                    return w[l].rearrange("(c p) n -> p c n", p=P)
                if name in cols:
                    at, n = cols[name]
                    w = w_in
                else:
                    kind, i = name
                    w, at = {"gate": (w_in, COL_GATE), "wo": (w_out, 0), "pq": (w_pq, 0)}[kind]
                    at, n = at + i * BANK, BANK
                return w[l].rearrange("(c p) n -> p c n", p=P)[:, :, at:at + n]

            def load_weights(s, name):
                n = s * NW + W_AT[name]
                if n >= W_SLOTS:
                    old = n - W_SLOTS
                    sp.wait_ge(proj_ready.sem, proj_ready.at(old // NW, W_CHUNKS[old % NW][1]))
                src = source(s // TILES, name)
                dst = weights[:, n % W_SLOTS, 0:src.shape[1] * src.shape[2]].rearrange("p (c n) -> p c n", c=src.shape[1])
                sp.dma_start(dst, src).then_inc(w_in_sem[n % W_SLOTS], 16)

            sp.dma_start(xs[:, 0, :], x[0]).then_inc(x_in, 16)
            sp.dma_start(ident[:, :], ident_in).then_inc(ident_sem, 16)
            load_mix_params(0)
            load_weights(0, "c")
            load_weights(0, "aq")
            sp.wait_ge(headrow_zero, 1)
            sp.dma_start(headrow[0:BUCKETS, 0:BIAS_HEADS], rel_bias).then_inc(head_in, 16)
            sp.dma_start(headrow[BUCKETS:BUCKETS + 2, :], maskrow_in).then_inc(head_in, 16)
            sp.dma_start(onehot, onehot_in).then_inc(head_in, 16)
            sp.dma_start(mixers[:, 2 * BANK:3 * BANK], bcast(lam_vecs)).then_inc(lam_in, 16)
            sp.dma_start(rope[:, :, :, :], rope_in.rearrange("(t p) a n -> p t a n", p=P)).then_inc(consts_in, 16)
            sp.dma_start(count[:, :], count_in).then_inc(consts_in, 16)
            sp.dma_start(iota[:, :], iota_in).then_inc(consts_in, 16)
            load_weights(0, "ak")
            load_weights(0, "av")
            sp.wait_ge(table_sb, 1)
            sp.dma_start(table_dram, table[:, 0:DISTS].unsqueeze(1).to_broadcast([BIAS_HEADS + 1, P, DISTS])).then_inc(table_out, 16)
            sp.wait_ge(table_out, 16)
            sp.dma_start(bias[:, :, :], bass.AP(tensor=table_dram.tensor, offset=P - 1,
                                                ap=[[DISTS - 1, P], [P * DISTS, BIAS_HEADS + 1], [1, SEQ]])).then_inc(bias_in, 16)
            load_ffn_params(0)
            sp.dma_start(xs[:, 1, :], x[1]).then_inc(x_in, 16)
            for s in range(STAGES):
                if s == TILES:
                    sp.wait_ge(y_ready.sem, y_ready.at(s - 1))
                    load_mix_params(1)
                for name, _ in W_CHUNKS[(4 if s == 0 else 0):]:
                    if s == TILES and name == ("gate", 0):
                        sp.wait_ge(route_ready.sem, route_ready.at(s - 1, 1))
                        sp.wait_ge(h2_ready.sem, h2_ready.at(s - 1))
                        load_ffn_params(1)
                    load_weights(s, name)
            sp.wait_ge(h_ready.sem, h_ready.at(STAGES - 1))
            sp.dma_start(gmix[:, :], bcast(g_final)).then_inc(final_params, 16)
            for t in range(TILES):
                sp.wait_ge(fin_row, t + 1)
                sp.dma_start(out[t], (hrow if t == 0 else h2row)[:, :]).then_inc(out_written, 16)
            sp.wait_ge(out_written, 16 * TILES)

        @block.gpsimd
        def _(pool):
            def head(s, table_rows, at, odd, heads_done, wait):
                if wait:
                    pool.wait_ge(rows_used, heads_done * TOPK - TOPK)
                    pool.sem_inc(pool_steps, 1)
                nc.gpsimd.tensor_copy(indexh[:, odd, :], index[:, s % 2, bass.ds(at, TOPK)]).then_inc(index_copied, 1)
                pool.wait_ge(index_copied, heads_done + 1)
                pool.sem_inc(pool_steps, 1)
                for k in range(TOPK):
                    if wait:
                        pool.wait_ge(rows_used, heads_done * TOPK + (k + 1 - RING))
                    elif odd * TOPK + k >= RING:
                        pool.wait_ge(rows_used, odd * TOPK + k + 1 - RING)
                    pool.sem_inc(pool_steps, 1)
                    pool.indirect_dma_start(rows[:, k % RING, :], None, table_rows,
                                            bass.IndirectOffsetOnAxis(ap=indexh[:, odd, k:k + 1], axis=0)).then_inc(row_in[k % RING], 16)

            for s in range(STAGES):
                pool.wait_ge(index_ready.sem, index_ready.at(s))
                for phase, table_rows in ((0, peer_u), (1, peer_v)):
                    before = (s * 2 + phase) * HEADS
                    if before == 0:
                        for odd in range(2):
                            head(s, table_rows, odd * TOPK, odd, odd, False)
                    with pool.Fori(1 if before == 0 else 0, HEADS // 2) as pair:
                        for odd in range(2):
                            head(s, table_rows, pair * (2 * TOPK) + odd * TOPK, odd, pair * 2 + (before + odd), True)

        @block.scalar
        def _(act):
            def copy(dst, src, scale=1.0):
                return nc.scalar.activation(dst, src, ACT.Copy, scale=scale)

            def evac(s, use, dst, src=None, scale=1.0):
                b = bank_of(s, use)
                act.wait_ge(proj_ready.sem, proj_ready.at(s, use))
                src = proj[b][:, 0:dst.free_size()] if src is None else src(proj[b])
                if len(dst.shape) == 3 and len(src.shape) == 2:
                    src = src.rearrange("p (a b) -> p a b", a=dst.shape[1])
                copy(dst, src, scale).then_inc(proj_free[b], 1)

            def root(s, i, n):
                act.wait_ge(mean_ready.sem, mean_ready.at(s, i))
                nc.scalar.activation(stat[:, 4:4 + n], stat[:, 0:n], ACT.Sqrt, bias=eps[:, 0:1])\
                    .then_inc(root_ready.sem, 1)

            def dense_first(s):
                t = s % TILES
                now = slice(t * P, (t + 1) * P)
                root(s, 0, 1)
                for i in range(2):
                    evac(s, HT0 + i, hT[:, 4 * i:4 * i + 4, :])
                evac(s, PC, crow)
                if s > 0:
                    act.wait_ge(s_ready.sem, s_ready.at(s - 1, GROUPS - 1))
                evac(s, AQ, qTA[:, :, :], scale=HD ** -0.5)
                root(s, 1, 2)
                if s % TILES == 0 and s > 0:
                    act.wait_ge(o_ready.sem, o_ready.at(s - 1, GROUPS - 1))
                evac(s, AK, kTA[:, :, now])
                evac(s, AV, vA[:, t, :])
                evac(s, CT, cT[:, :, :])
                for i in range(2):
                    evac(s, CQ0 + i, qrow[:, 3 * i:3 * i + 3, :], scale=C_QK ** -0.5)
                for i in range(2):
                    b = bank_of(s, CKV0 + i)
                    act.wait_ge(proj_ready.sem, proj_ready.at(s, CKV0 + i))
                    src = proj[b][:, 0:3 * P].rearrange("p (h c) -> p h c", h=3)
                    copy(krow[:, 3 * i:3 * i + 3, 0:HD], src[:, :, 0:HD])
                    copy(vC[:, t, 3 * i * HD:3 * (i + 1) * HD].rearrange("p (h c) -> p h c", h=3), src[:, :, HD:P])\
                        .then_inc(proj_free[b], 1)
                evac(s, BQ, qTB[:, :, :], scale=HD ** -0.5)
                evac(s, BK, kTB[:, :, now])
                evac(s, BV, vB[:, t, :])
                for i, (h0, h1) in enumerate(((0, 4), (4, 6))):
                    evac(s, CQT0 + i, qTC[:, h0:h1, :], src=lambda pb, n=(h1 - h0) * P: pb[0:C_QK, 0:n])
                for i, (h0, h1) in enumerate(((0, 4), (4, 6))):
                    evac(s, CKT0 + i, kTC[:, h0:h1, now], src=lambda pb, n=(h1 - h0) * P: pb[0:C_QK, 0:n])

                nk = (t + 1) * P
                for i in range(GROUPS + 2):
                    if i < GROUPS:
                        exps(s, i, nk)
                    if i % 2 == 1:
                        g = i // 2
                        evac(s, GATE0 + g, gates[:, g * BANK:(g + 1) * BANK])
                    if 0 <= i - 1 < GROUPS:
                        transposed(s, i - 1, nk)
                root(s, 2, 4)

            def exps(s, g, nk):
                b = g % 2
                act.wait_ge(neg_ready.sem, neg_ready.at(s, g))
                if g >= 2:
                    act.wait_ge(pT_ready.sem, pT_ready.at(s, g - 2))
                for m in range(2):
                    acc = {} if kind_of(g)[0] == "A" else {"accum_out": denom[:, b, m:m + 1]}
                    last = nc.scalar.activation(probs[:, b, m, 0:nk], logits[:, b, m, 0:nk], ACT.Exp,
                                                bias=negmax[:, b, m:m + 1], **acc)
                last.then_inc(e_ready.sem, 1)

            def transposed(s, g, nk):
                n = nk if kind_of(g)[0] == "B" else 2 * nk
                act.wait_ge(pT_ready.sem, pT_ready.at(s, g))
                if g >= 2:
                    act.wait_ge(o_ready.sem, o_ready.at(s, g - 2))
                copy(probsT[:, g % 2, 0:n], psT[:, 0:n]).then_inc(pTs_ready.sem, 1)

            def gelu(s):
                act.wait_ge(rows_used, row_step(s, 1, 0))
                nc.scalar.activation(coef[:, :], acts[:, :], ACT.Gelu).then_inc(gelu_ready.sem, 1)

            def dense_second(s):
                act.wait_ge(proj_free[bank_of(s, GATE0 + 5)], freed(s, GATE0 + 5))
                act.wait_ge(proj_free[bank_of(s, GATE0 + 4)], freed(s, GATE0 + 4))
                nc.scalar.activation(gates[:, :], gates[:, :], ACT.Sigmoid).then_inc(sig_ready.sem, 1)
                for i, (b0, b1) in enumerate(((0, 4), (4, 8), (8, 10))):
                    evac(s, YT0 + i, yT[:, b0:b1, :])
                for i in range(2):
                    evac(s, MT0 + i, hT[:, 4 * i:4 * i + 4, :])
                root(s, 3, 1)
                for i in range(2):
                    evac(s, H2T0 + i, hT[:, 4 * i:4 * i + 4, :])
                for i in range(2):
                    evac(s, PQ0 + i, pqT[:, 4 * i:4 * i + 4, :])
                act.wait_ge(best_ready.sem, best_ready.at(s))
                nc.scalar.activation(pickw[:, s % 2, :], pickw[:, s % 2, :], ACT.Exp).then_inc(bexp_ready.sem, 1)

            act.wait_ge(table_ps, 1)
            copy(table, psO[0:BIAS_HEADS + 1, :]).then_inc(table_sb, 1)
            act.wait_ge(lam_sums, 1)
            nc.scalar.activation(lams[:, :, :], lams[:, :, :], ACT.Exp).then_inc(lam_exps, 1)
            act.wait_ge(eps_set, 1)
            for s in range(STAGES):
                dense_first(s)
                if s > 0:
                    gelu(s - 1)
                dense_second(s)
            for t in range(TILES):
                if t == TILES - 1:
                    gelu(STAGES - 1)
                act.wait_ge(fin_mean, t + 1)
                nc.scalar.activation(stat[:, 4:5], stat[:, 0:1], ACT.Sqrt, bias=eps[:, 0:1]).then_inc(fin_root, 1)

        @block.vector
        def _(dve):
            done = [0]

            def noted(ins):
                done[0] += 1
                return ins.then_inc(dve_done, 1)

            def settle():
                dve.wait_ge(dve_done, done[0])

            def link(ins):
                noted(ins)
                settle()

            V = nc.vector

            def mean_square(dst, src, junk, n):
                return V.scalar_tensor_tensor(out=junk, in0=src, scalar=1.0 / n, in1=src, op0=ALU.mult, op1=ALU.mult,
                                              accum_out=dst)

            def dot_step(s, slot, k, n):
                V.scalar_tensor_tensor(out=rows[:, slot, :], in0=rows[:, slot, :], scalar=1.0, in1=h2row[:, :],
                                       op0=ALU.mult, op1=ALU.mult, accum_out=acts[:, bass.ds(k, 1)])\
                    .then_inc(rows_used, 1)

            def add_step(s, slot, k, n):
                dve.wait_ge(rows_used, n)
                t = s % TILES
                V.scalar_tensor_tensor(out=xs[:, t, :], in0=rows[:, slot, :], scalar=coef[:, bass.ds(k, 1)],
                                       in1=xs[:, t, :], op0=ALU.mult, op1=ALU.add).then_inc(rows_used, 1)

            class Retrieval:

                def __init__(self, s, phase):
                    self.s, self.phase, self.k = s, phase, 0

                def head(self, h, slots=range(TOPK)):
                    step = (dot_step, add_step)[self.phase]
                    for k in slots:
                        fills = h * (TOPK // RING) + (row_step(self.s, self.phase, k) // RING + 1)
                        dve.wait_ge(row_in[k % RING], fills * 16)
                        step(self.s, k % RING, h * TOPK + k, h * TOPK + (row_step(self.s, self.phase, 0) + k))

                def part(self, n):
                    n = min(n, PICKS - self.k)
                    while n > 0:
                        h, at = divmod(self.k, TOPK)
                        m = min(n, TOPK - at)
                        self.head(h, range(at, at + m))
                        self.k, n = self.k + m, n - m

                def heads(self, n):
                    h = self.k // TOPK
                    assert self.k % TOPK == 0
                    if n > 0:
                        with dve.Fori(h, h + n) as i:
                            self.head(i)
                        self.k += n * TOPK

                def rest(self):
                    self.part(-self.k % TOPK)
                    self.heads((PICKS - self.k) // TOPK)

            class Nothing:
                def part(self, n):
                    pass

                heads = part

            def coefficients(s):
                dve.wait_ge(gelu_ready.sem, gelu_ready.at(s))
                V.tensor_tensor(coef[:, :], coef[:, :], pickw[:, s % 2, :], ALU.mult).then_inc(coef_ready.sem, 1)
                dve.wait_ge(coef_ready.sem, coef_ready.at(s))

            def dense_first(s, fill):
                l, t = divmod(s, TILES)
                nk = (t + 1) * P
                if s == 0:
                    dve.wait_ge(x_in, 16)
                if s == 1:
                    dve.wait_ge(x_in, 32)
                if s >= TILES:
                    dve.wait_ge(rows_used, row_step(s - TILES + 1, 0, 0))
                mean_square(stat[:, 0:1], xs[:, t, :], hrow[:, :], D).then_inc(mean_ready.sem, 1)
                dve.wait_ge(mix_params, 96 * (l + 1))
                dve.wait_ge(root_ready.sem, root_ready.at(s, 0))
                link(V.reciprocal(stat[:, 8:9], stat[:, 4:5]))
                V.scalar_tensor_tensor(out=hrow[:, :], in0=xs[:, t, :], scalar=stat[:, 8:9], in1=gmix[:, :],
                                       op0=ALU.mult, op1=ALU.mult).then_inc(h_ready.sem, 1)
                if t == 0:
                    lam_init = 0.8 - 0.6 * math.exp(-0.3 * l)
                    link(V.tensor_scalar(gsub[:, :], gsub[:, :], 1.0 - lam_init, None, ALU.mult))
                fill.part(10)
                dve.wait_ge(proj_free[bank_of(s, PC)], freed(s, PC))
                mean_square(stat[:, 0:1], crow[:, 0:Q_RANK], cnorm[:, 0:Q_RANK], Q_RANK)
                mean_square(stat[:, 1:2], crow[:, Q_RANK:Q_RANK + KV_RANK], cnorm[:, Q_RANK:], KV_RANK)\
                    .then_inc(mean_ready.sem, 1)
                dve.wait_ge(root_ready.sem, root_ready.at(s, 1))
                link(V.reciprocal(stat[:, 8:10], stat[:, 4:6]))
                V.scalar_tensor_tensor(out=cnorm[:, 0:Q_RANK], in0=crow[:, 0:Q_RANK], scalar=stat[:, 8:9],
                                       in1=gcq[:, :], op0=ALU.mult, op1=ALU.mult)
                V.scalar_tensor_tensor(out=cnorm[:, Q_RANK:], in0=crow[:, Q_RANK:Q_RANK + KV_RANK],
                                       scalar=stat[:, 9:10], in1=gckv[:, :], op0=ALU.mult, op1=ALU.mult)\
                    .then_inc(cnorm_ready.sem, 1)
                fill.part(14)

                if s == 0:
                    dve.wait_ge(consts_in, 48)

                def rotate(x1, x2, o1, o2, heads):
                    n = heads * 16
                    r = [rot[:, j, 0:n].rearrange("p (h c) -> p h c", h=heads) for j in range(4)]
                    cos, sin = (rope[:, t, j, 0:n].rearrange("p (h c) -> p h c", h=heads) for j in range(2))
                    for dst, a, f in ((r[0], x1, cos), (r[1], x2, sin), (r[2], x1, sin), (r[3], x2, cos)):
                        noted(V.tensor_tensor(dst, a, f, ALU.mult))
                    settle()
                    noted(V.tensor_tensor(o1, r[0], r[1], ALU.subtract))
                    return V.tensor_tensor(o2, r[2], r[3], ALU.add)

                c0 = Q_RANK + KV_RANK
                one = lambda ap: ap.rearrange("p (h c) -> p h c", h=1)
                link(rotate(one(crow[:, c0:c0 + 16]), one(crow[:, c0 + 16:c0 + 32]),
                            one(krot[:, 0:16]), one(krot[:, 16:32]), 1))
                V.tensor_copy(krow[:, :, HD:C_QK], krot[:, :].unsqueeze(1).to_broadcast([P, C_HEADS, ROPE]))\
                    .then_inc(krope_ready.sem, 1)
                for i in range(2):
                    dve.wait_ge(proj_free[bank_of(s, CQ0 + i)], freed(s, CQ0 + i))
                q1, q2 = qrow[:, :, HD:HD + 16], qrow[:, :, HD + 16:C_QK]
                rotate(q1, q2, q1, q2, C_HEADS).then_inc(qrope_ready.sem, 1)
                fill.part(16)

                for i in range(GROUPS + 2):
                    if i < GROUPS:
                        masked(s, i, t, nk)
                    if 0 <= i - 1 < GROUPS:
                        weigh(s, i - 1, l, nk)
                    if 0 <= i - 2 < GROUPS:
                        outputs(s, i - 2)
                    if i - 2 == 6:
                        dve.wait_ge(o_used.sem, o_used.at(s, 6))
                        for h in range(B_HEADS):
                            last = mean_square(stat[:, h:h + 1], y[:, (3 + h) * P:(4 + h) * P], mixers[:, (10 + h) * P:(11 + h) * P], P)
                        last.then_inc(mean_ready.sem, 1)
                    fill.part(7)
                dve.wait_ge(root_ready.sem, root_ready.at(s, 2))
                link(V.reciprocal(stat[:, 8:12], stat[:, 4:8]))
                for h in range(B_HEADS):
                    yh = y[:, (3 + h) * P:(4 + h) * P]
                    last = V.scalar_tensor_tensor(out=yh, in0=yh, scalar=stat[:, 8 + h:9 + h], in1=gsub[:, :],
                                                  op0=ALU.mult, op1=ALU.mult)
                last.then_inc(y_ready.sem, 1)

            def masked(s, g, t, nk):
                b, (kind, j) = g % 2, kind_of(g)
                first = P * (TILES - 1 - t)
                if s == 0 and g == 0:
                    dve.wait_ge(bias_in, 16)
                if kind == "A":
                    add = bias[:, 2 * j:2 * j + 2, first:first + nk]
                else:
                    row = A_HEADS + j if kind == "B" else BIAS_HEADS
                    add = bias[:, row, first:first + nk].unsqueeze(1).to_broadcast([P, 2, nk])
                dve.wait_ge(s_ready.sem, s_ready.at(s, g))
                if g >= 2:
                    dve.wait_ge(e_ready.sem, e_ready.at(s, g - 2))
                raw = sc[b][:, :].rearrange("p (m n) -> p m n", m=2)[:, :, 0:nk]
                link(V.tensor_tensor(logits[:, b, :, 0:nk], raw, add, ALU.add))
                V.tensor_reduce(negmax[:, b, :], logits[:, b, :, 0:nk], AX.X, ALU.max, negate=True)\
                    .then_inc(neg_ready.sem, 1)

            def weigh(s, g, l, nk):
                b, (kind, _) = g % 2, kind_of(g)
                dve.wait_ge(e_ready.sem, e_ready.at(s, g))
                if g >= 2:
                    dve.wait_ge(o_used.sem, o_used.at(s, g - 2))
                if kind == "A":
                    first = SEQ - nk
                    for m in range(2):
                        last = V.scalar_tensor_tensor(out=probs[:, b, m, 0:nk], in0=probs[:, b, m, 0:nk], scalar=1.0,
                                                      in1=count[:, first:first + nk], op0=ALU.mult, op1=ALU.mult,
                                                      accum_out=denom[:, b, m:m + 1])
                    link(last)
                    V.reciprocal(recip[:, b, :], denom[:, b, :]).then_inc(p_ready.sem, 1)
                elif kind == "B":
                    link(V.reciprocal(recip[:, b, :], denom[:, b, :]))
                    link(V.scalar_tensor_tensor(out=lamr[:, :], in0=denom[:, b, 0:1], scalar=recip[:, b, 1:2],
                                                in1=neglam[:, l:l + 1], op0=ALU.mult, op1=ALU.mult))
                    V.scalar_tensor_tensor(out=probs[:, b, 0, 0:nk], in0=probs[:, b, 1, 0:nk], scalar=lamr[:, 0:1],
                                           in1=probs[:, b, 0, 0:nk], op0=ALU.mult, op1=ALU.add)\
                        .then_inc(p_ready.sem, 1)
                else:
                    V.reciprocal(recip[:, b, :], denom[:, b, :]).then_inc(p_ready.sem, 1)

            def outputs(s, g):
                b, (kind, _) = g % 2, kind_of(g)
                dve.wait_ge(o_ready.sem, o_ready.at(s, g))
                dst = y[:, g * P:(g + 1) * P]
                if kind == "B":
                    V.tensor_scalar(dst, psO[:, 0:P], recip[:, b, 0:1], None, ALU.mult).then_inc(o_used.sem, 1)
                else:
                    V.tensor_tensor(dst.rearrange("p (m c) -> p m c", m=2),
                                    psO[:, 0:P].rearrange("p (m c) -> p m c", m=2),
                                    recip[:, b, :].unsqueeze(2).to_broadcast([P, 2, HD]), ALU.mult)\
                        .then_inc(o_used.sem, 1)

            def dense_second(s, fill):
                l, t = divmod(s, TILES)
                dve.wait_ge(sig_ready.sem, sig_ready.at(s))
                fill.part(8)
                for half in range(2):
                    cols = slice(half * BANK, (half + 1) * BANK)
                    for br in range(3):
                        use = BR0 + 3 * half + br
                        b = bank_of(s, use)
                        gate = gates[:, br * D + half * BANK:br * D + (half + 1) * BANK]
                        dve.wait_ge(proj_ready.sem, proj_ready.at(s, use))
                        V.tensor_tensor(mix[:, cols] if br == 0 else tmp, proj[b][:, :], gate, ALU.mult)\
                            .then_inc(proj_free[b], 1)
                        if br > 0:
                            dve.wait_ge(proj_free[b], freed(s, use))
                            add = V.tensor_tensor(mix[:, cols], mix[:, cols], tmp, ALU.add)
                            if br == 2:
                                add.then_inc(mix_ready.sem, 1)
                            else:
                                link(add)
                        else:
                            dve.wait_ge(proj_free[b], freed(s, use))
                        fill.part(3)
                for half in range(2):
                    b = bank_of(s, WO0 + half)
                    xh = xs[:, t, half * BANK:(half + 1) * BANK]
                    dve.wait_ge(proj_ready.sem, proj_ready.at(s, WO0 + half))
                    V.tensor_tensor(xh, proj[b][:, :], xh, ALU.add).then_inc(proj_free[b], 1)
                    dve.wait_ge(proj_free[b], freed(s, WO0 + half))
                mean_square(stat[:, 0:1], xs[:, t, :], h2row[:, :], D).then_inc(mean_ready.sem, 1)
                dve.wait_ge(ffn_params, 32 * (l + 1))
                fill.part(1)
                dve.wait_ge(root_ready.sem, root_ready.at(s, 3))
                link(V.reciprocal(stat[:, 8:9], stat[:, 4:5]))
                V.scalar_tensor_tensor(out=h2row[:, :], in0=xs[:, t, :], scalar=stat[:, 8:9], in1=gffn[:, :],
                                       op0=ALU.mult, op1=ALU.mult).then_inc(h2_ready.sem, 1)
                fill.part(10)

                for buf in range(2):
                    dve.wait_ge(route_ready.sem, route_ready.at(s, buf))
                    for hh in range(4):
                        lists = [(4 * buf + hh) * 2 + p for p in range(2)]
                        raws = [sc[buf][:, p * BANK + hh * KEYS:p * BANK + (hh + 1) * KEYS] for p in range(2)]
                        for j, raw in zip(lists, raws):
                            noted(V.max(tops[:, j, 0:8], raw))
                        settle()
                        for j, raw in zip(lists, raws):
                            V.max_index(topi[:, j, 0:8], tops[:, j, 0:8], raw)
                            noted(V.match_replace(scores[:, j, :], tops[:, j, 0:8], raw, NEG))
                        settle()
                        for j in lists:
                            noted(V.max(tops[:, j, 8:16], scores[:, j, :]))
                        settle()
                        for j in lists:
                            noted(V.max_index(topi[:, j, 8:16], tops[:, j, 8:16], scores[:, j, :]))
                        fill.part(4)
                settle()
                noted(V.tensor_copy(topf[:, :, :], topi[:, :, :]))
                pairs = tops[:, :, :].rearrange("p (h two) a -> p h two a", two=2)
                c4 = cand.rearrange("p (h a b) -> p h a b", h=HEADS, a=TOPK)
                full = [P, HEADS, TOPK, TOPK]
                link(V.tensor_tensor(c4, pairs[:, :, 0, :].unsqueeze(3).to_broadcast(full),
                                     pairs[:, :, 1, :].unsqueeze(2).to_broadcast(full), ALU.add))
                for h0 in range(0, HEADS, 2):
                    two = [(h, cand[:, h * 256:(h + 1) * 256]) for h in (h0, h0 + 1)]
                    for h, c in two:
                        noted(V.max(best[:, h, 0:8], c))
                    settle()
                    for h, c in two:
                        link(V.max_index(bestpos[:, h, 0:8], best[:, h, 0:8], c))
                        noted(V.match_replace(c, best[:, h, 0:8], c, NEG))
                    settle()
                    for h, c in two:
                        noted(V.max(best[:, h, 8:16], c))
                    settle()
                    for h, c in two:
                        noted(V.max_index(bestpos[:, h, 8:16], best[:, h, 8:16], c))
                    fill.part(4)
                settle()
                pw = pickw[:, s % 2, :].rearrange("p (h k) -> p h k", h=HEADS)
                V.tensor_tensor(pw, best[:, :, :], best[:, :, 0:1].to_broadcast([P, HEADS, TOPK]), ALU.subtract)\
                    .then_inc(best_ready.sem, 1)
                flatpos = bestpos[:, :, :].rearrange("p h k -> p (h k)")
                noted(V.tensor_scalar(pos[:, 0, :], flatpos, 4, None, ALU.logical_shift_right))
                noted(V.tensor_scalar(pos[:, 1, :], flatpos, TOPK - 1, None, ALU.bitwise_and))
                settle()
                link(V.tensor_copy(posf[:, :, :], pos[:, :, :]))
                index_pairs = topf[:, :, :].rearrange("p (h two) a -> p h two a", two=2)
                places = iota[:, :].unsqueeze(1).to_broadcast([P, PICKS, TOPK])
                c3 = cand.rearrange("p (k a) -> p k a", a=TOPK)
                for half in range(2):
                    link(V.tensor_tensor(c3, posf[:, half, :].unsqueeze(2).to_broadcast([P, PICKS, TOPK]), places,
                                         ALU.is_equal))
                    link(V.tensor_tensor(c4, c4, index_pairs[:, :, half, :].unsqueeze(2).to_broadcast(full), ALU.mult))
                    link(V.tensor_reduce(part[:, half, :], c3, AX.X, ALU.add))
                link(V.tensor_scalar(part[:, 0, :], part[:, 0, :], float(KEYS), float(l * EXPERTS), ALU.mult, ALU.add))
                V.tensor_tensor(index[:, s % 2, :], part[:, 0, :], part[:, 1, :], ALU.add).then_inc(index_ready.sem, 1)
                dve.wait_ge(bexp_ready.sem, bexp_ready.at(s))
                link(V.tensor_reduce(gsum[:, 0, :], pw, AX.X, ALU.add))
                link(V.reciprocal(gsum[:, 1, :], gsum[:, 0, :]))
                link(V.tensor_tensor(pw, pw, gsum[:, 1, :].unsqueeze(2).to_broadcast([P, HEADS, TOPK]), ALU.mult))

            def final_norm(t):
                dst = (hrow if t == 0 else h2row)[:, :]
                mean_square(stat[:, 0:1], xs[:, t, :], dst, D).then_inc(fin_mean, 1)
                if t == 0:
                    dve.wait_ge(final_params, 16)
                dve.wait_ge(fin_root, t + 1)
                link(V.reciprocal(stat[:, 8:9], stat[:, 4:5]))
                V.scalar_tensor_tensor(out=dst, in0=xs[:, t, :], scalar=stat[:, 8:9], in1=gmix[:, :],
                                       op0=ALU.mult, op1=ALU.mult).then_inc(fin_row, 1)

            V.memset(headrow[:, :], 0.0).then_inc(headrow_zero, 1)
            V.memset(eps[:, :], EPS).then_inc(eps_set, 1)
            dve.wait_ge(lam_in, 16)
            for l in range(DEPTH):
                for j in range(2):
                    junk = (2 * l + j) * HD
                    last = V.scalar_tensor_tensor(out=tmp[:, junk:junk + HD], in0=lamv[:, l, 2 * j, :], scalar=1.0,
                                                  in1=lamv[:, l, 2 * j + 1, :], op0=ALU.mult, op1=ALU.mult,
                                                  accum_out=lams[:, l, j:j + 1])
            last.then_inc(lam_sums, 1)
            dve.wait_ge(lam_exps, 1)
            for l in range(DEPTH):
                link(V.tensor_tensor(neglam[:, l:l + 1], lams[:, l, 1:2], lams[:, l, 0:1], ALU.subtract))
                link(V.tensor_scalar(neglam[:, l:l + 1], neglam[:, l:l + 1], -(0.8 - 0.6 * math.exp(-0.3 * l)), None,
                                     ALU.add))
            dense_first(0, Nothing())
            dense_second(0, Nothing())
            for s in range(1, STAGES):
                dots = Retrieval(s - 1, 0)
                dense_first(s, dots)
                dots.rest()
                coefficients(s - 1)
                adds = Retrieval(s - 1, 1)
                dense_second(s, adds)
                adds.rest()
            dve.wait_ge(rows_used, row_step(STAGES - 1, 0, 0))
            final_norm(0)
            dots = Retrieval(STAGES - 1, 0)
            dots.heads(HEADS)
            coefficients(STAGES - 1)
            adds = Retrieval(STAGES - 1, 1)
            adds.heads(HEADS)
            dve.wait_ge(rows_used, row_step(STAGES, 0, 0))
            final_norm(1)

        @block.tensor
        def _(pe):
            def begin(s, use):
                b = bank_of(s, use)
                n = freed(s, use) - 1
                if n > 0:
                    pe.wait_ge(proj_free[b], n)
                return proj[b]

            def end(last):
                last.then_inc(proj_ready.sem, 1)

            def evacuated(s, use):
                pe.wait_ge(proj_free[bank_of(s, use)], freed(s, use))

            def w_arrived(s, name):
                n = s * NW + W_AT[name]
                pe.wait_ge(w_in_sem[n % W_SLOTS], 16 * (n // W_SLOTS + 1))

            def w_chunk(s, name, kc, width):
                n = s * NW + W_AT[name]
                return weights[:, n % W_SLOTS, 0:kc * width].rearrange("p (c n) -> p c n", c=kc)

            def transposes(s, use, sources, rows_out=P):
                bank = begin(s, use)
                for j, src in enumerate(sources):
                    last = nc.tensor.transpose(bank[0:rows_out, j * P:(j + 1) * P], src, ident[:, :])
                end(last)

            def product(s, use, lhs, rhs, width, parts=((0, None),)):
                bank = begin(s, use)
                kc = len(lhs)
                for c in range(kc):
                    last = nc.tensor.matmul(bank[:, 0:width], lhs[c], rhs[c], start=(c == 0), stop=(c == kc - 1))
                end(last)

            def product_T(s, use, w, blocks):
                bank = begin(s, use)
                for j in range(blocks):
                    for c in range(KC):
                        last = nc.tensor.matmul(bank[:, j * P:(j + 1) * P], w[:, c, j * P:(j + 1) * P], hT[:, c, :],
                                                start=(c == 0), stop=(c == KC - 1))
                end(last)

            def row_chunk(s, use, name, width):
                w_arrived(s, name)
                w = w_chunk(s, name, KC, width)
                product(s, use, [hT[:, c, :] for c in range(KC)], [w[:, c, :] for c in range(KC)], width)

            def transposed_chunk(s, use, name, blocks):
                w_arrived(s, name)
                product_T(s, use, w_chunk(s, name, KC, blocks * P), blocks)

            def gate_half(s, i):
                g, second = divmod(i, 2)
                if not second:
                    w_arrived(s, ("gate", g))
                    begin(s, GATE0 + g)
                w = w_chunk(s, ("gate", g), KC, BANK)
                for c in range(4 * second, 4 * second + 4):
                    last = nc.tensor.matmul(proj[bank_of(s, GATE0 + g)][:, :], hT[:, c, :], w[:, c, :],
                                            start=(c == 0), stop=(c == KC - 1))
                if second:
                    end(last)

            def dense_first(s):
                t = s % TILES
                nk = (t + 1) * P
                nb = t + 1
                pe.wait_ge(h_ready.sem, h_ready.at(s))
                for i in range(2):
                    transposes(s, HT0 + i, [hrow[:, c * P:(c + 1) * P] for c in range(4 * i, 4 * i + 4)])
                for i in range(2):
                    evacuated(s, HT0 + i)
                row_chunk(s, PC, "c", C_WIDTH)
                transposed_chunk(s, AQ, "aq", 3)
                transposed_chunk(s, AK, "ak", 3)
                row_chunk(s, AV, "av", A_HEADS * HD)
                pe.wait_ge(cnorm_ready.sem, cnorm_ready.at(s))
                transposes(s, CT, [cnorm[:, j * P:(j + 1) * P] for j in range(3)])
                evacuated(s, CT)
                for i in range(2):
                    n = 3 * C_QK
                    product(s, CQ0 + i, [cT[:, c, :] for c in range(2)],
                            [wuq[:, c, i * n:(i + 1) * n] for c in range(2)], n)
                for i in range(2):
                    n = 3 * P
                    product(s, CKV0 + i, [cT[:, 2, :]], [wukv[:, i * n:(i + 1) * n]], n)
                transposed_chunk(s, BQ, "bq", B_HEADS)
                transposed_chunk(s, BK, "bk", B_HEADS)
                row_chunk(s, BV, "bv", B_HEADS * P)
                pe.wait_ge(qrope_ready.sem, qrope_ready.at(s))
                for i, (h0, h1) in enumerate(((0, 4), (4, 6))):
                    transposes(s, CQT0 + i, [qrow[:, h, :] for h in range(h0, h1)], C_QK)
                pe.wait_ge(krope_ready.sem, krope_ready.at(s))
                for i in range(2):
                    evacuated(s, CKV0 + i)
                for i, (h0, h1) in enumerate(((0, 4), (4, 6))):
                    transposes(s, CKT0 + i, [krow[:, h, :] for h in range(h0, h1)], C_QK)

                for i in range(GROUPS + 2):
                    if i < GROUPS:
                        score(s, i, nk)
                    gate_half(s, i)
                    if 0 <= i - 1 < GROUPS:
                        transpose_probs(s, i - 1, nb)
                    if 0 <= i - 2 < GROUPS:
                        times_v(s, i - 2, nb)

            def score(s, g, nk):
                b, (kind, j) = g % 2, kind_of(g)
                if g == 0:
                    evacuated(s, AK)
                if g == 3:
                    evacuated(s, BK)
                if g == 7:
                    evacuated(s, CKT0)
                    evacuated(s, CKT1)
                if g >= 2:
                    pe.wait_ge(neg_ready.sem, neg_ready.at(s, g - 2))
                elif s > 0:
                    pe.wait_ge(index_ready.sem, index_ready.at(s - 1))
                for m in range(2):
                    half = slice(m * HD, (m + 1) * HD)
                    if kind == "A":
                        q, k = qTA[half, j, :], kTA[half, j, 0:nk]
                    elif kind == "B":
                        q, k = qTB[half, j, :], kTB[half, j, 0:nk]
                    else:
                        q, k = qTC[:, 2 * j + m, :], kTC[:, 2 * j + m, 0:nk]
                    last = nc.tensor.matmul(sc[b][:, m * BANK:m * BANK + nk], q, k, start=True, stop=True)
                last.then_inc(s_ready.sem, 1)

            def transpose_probs(s, g, nb):
                b = g % 2
                maps = 1 if kind_of(g)[0] == "B" else 2
                pe.wait_ge(p_ready.sem, p_ready.at(s, g))
                if g > 0 or s > 0:
                    pe.wait_ge(pTs_ready.sem, pTs_ready.at(s, g - 1))
                for m in range(maps):
                    for c in range(nb):
                        at = (m * nb + c) * P
                        last = nc.tensor.transpose(psT[:, at:at + P], probs[:, b, m, c * P:(c + 1) * P], ident[:, :])
                last.then_inc(pT_ready.sem, 1)

            def times_v(s, g, nb):
                b, (kind, j) = g % 2, kind_of(g)
                pe.wait_ge(pTs_ready.sem, pTs_ready.at(s, g))
                if g > 0 or s > 0:
                    pe.wait_ge(o_used.sem, o_used.at(s, g - 1))
                else:
                    pe.wait_ge(table_sb, 1)
                for m in range(1 if kind == "B" else 2):
                    width = 2 * HD if kind == "B" else HD
                    for c in range(nb):
                        v = {"A": vA, "B": vB, "C": vC}[kind][:, c, (j if kind == "B" else 2 * j + m) * width:][:, 0:width]
                        at = (m * nb + c) * P
                        last = nc.tensor.matmul(psO[:, m * HD:m * HD + width], probsT[:, b, at:at + P], v,
                                                start=(c == 0), stop=(c == nb - 1))
                last.then_inc(o_ready.sem, 1)

            def dense_second(s):
                pe.wait_ge(y_ready.sem, y_ready.at(s))
                for i, (b0, b1) in enumerate(((0, 4), (4, 8), (8, 10))):
                    transposes(s, YT0 + i, [y[:, b * P:(b + 1) * P] for b in range(b0, b1)])
                for i in range(3):
                    evacuated(s, YT0 + i)
                branches = (("wa", 0, 3), ("wb", 3, 4), ("wc", 7, 3))
                for half in range(2):
                    for br, (name, b0, kc) in enumerate(branches):
                        if half == 0:
                            w_arrived(s, name)
                        w = w_chunk(s, name, kc, D)
                        product(s, BR0 + 3 * half + br, [yT[:, b0 + c, :] for c in range(kc)],
                                [w[:, c, half * BANK:(half + 1) * BANK] for c in range(kc)], BANK)
                for i in range(2):
                    pe.wait_ge(mix_ready.sem, mix_ready.at(s, i))
                    transposes(s, MT0 + i, [mix[:, c * P:(c + 1) * P] for c in range(4 * i, 4 * i + 4)])
                for i in range(2):
                    evacuated(s, MT0 + i)
                for i in range(2):
                    row_chunk(s, WO0 + i, ("wo", i), BANK)
                pe.wait_ge(h2_ready.sem, h2_ready.at(s))
                for i in range(2):
                    transposes(s, H2T0 + i, [h2row[:, c * P:(c + 1) * P] for c in range(4 * i, 4 * i + 4)])
                for i in range(2):
                    evacuated(s, H2T0 + i)
                for i in range(2):
                    transposed_chunk(s, PQ0 + i, ("pq", i), 4)
                for buf in range(2):
                    evacuated(s, PQ0 + buf)
                    for hh in range(4):
                        h = 4 * buf + hh
                        for p in range(2):
                            half = slice(p * HD, (p + 1) * HD)
                            at = p * BANK + hh * KEYS
                            last = nc.tensor.matmul(sc[buf][:, at:at + KEYS], pqT[half, h, :], keys[half, h, :],
                                                    start=True, stop=True)
                    last.then_inc(route_ready.sem, 1)

            pe.wait_ge(ident_sem, 16)
            pe.wait_ge(head_in, 48)
            nc.tensor.matmul(psO[0:BIAS_HEADS + 1, :], headrow[:, :], onehot, start=True, stop=True)\
                .then_inc(table_ps, 1)
            for s in range(STAGES):
                dense_first(s)
                dense_second(s)


def shape_constants():
    import numpy as np
    ident = np.eye(P, dtype=np.float32)
    dist = SEQ - 1 - np.arange(BANK)
    exact = BUCKETS // 2
    nf = np.maximum(dist, exact).astype(np.float32)
    large = exact + (np.log(nf / np.float32(exact)) / np.float32(math.log(MAX_DISTANCE / exact))
                     * np.float32(BUCKETS - exact)).astype(np.int32)
    bucket = np.where(np.maximum(dist, 0) < exact, np.maximum(dist, 0), np.minimum(large, BUCKETS - 1))
    occurs = lambda d: sum((d >= 0) & (d <= window) & (d % dilation == 0) for window, dilation in A_CONFIGS)
    onehot = np.zeros((BUCKETS + 2, BANK), np.float32)
    onehot[bucket, np.arange(BANK)] = dist >= 0
    onehot[BUCKETS] = np.where(dist >= 0, 0.0, NEG)
    onehot[BUCKETS + 1] = np.where((dist >= 0) & (occurs(dist) == 0), NEG, 0.0)
    maskrow = np.ones((2, BIAS_HEADS + 1), np.float32)
    maskrow[1, A_HEADS:] = 0.0
    count = occurs(P + np.arange(P)[:, None] - np.arange(SEQ)[None, :]).astype(np.float32)
    half = ROPE // 2
    inv = np.float32(10000.0) ** (-np.arange(half, dtype=np.float32) / np.float32(half))
    ang = np.arange(SEQ, dtype=np.float32)[:, None] * inv[None, :]
    rope = np.stack([np.tile(np.cos(ang), 7), np.tile(np.sin(ang), 7)], 1).astype(np.float32)
    iota = np.tile(np.arange(TOPK, dtype=np.float32), (P, 1))
    return ident, onehot, maskrow, count, rope, iota


def kernel(**inputs):
    import numpy as np
    import concourse.bacc as bacc
    from concourse.bass_utils import run_bass_kernel_spmd

    a = {k: np.asarray(v) for k, v in inputs.items()}
    ident, onehot, maskrow, count, rope, iota = shape_constants()
    laid = {
        "x": a["x"].reshape(TILES, P, D), "rel_bias": a["rel_bias"], "w_in": a["w_in"], "g_mix": a["g_mix"],
        "w_uq": a["w_uq"], "g_cq": a["g_cq"], "w_ukv": a["w_ukv"], "g_ckv": a["g_ckv"],
        "lam_vecs": np.stack([a["lam_q1"], a["lam_k1"], a["lam_q2"], a["lam_k2"]], 1).reshape(-1),
        "g_subln": a["g_subln"], "w_a": a["w_branch_a"], "w_b": a["w_branch_b"], "w_c": a["w_branch_c"],
        "w_out": a["w_out"], "g_ffn": a["g_ffn"], "w_pq": a["w_peer_q"],
        "keysT": a["peer_sub_keys"].transpose(0, 2, 4, 1, 3).reshape(DEPTH, P, HEADS * KEYS),
        "peer_u": a["peer_u"].reshape(DEPTH * EXPERTS, D), "peer_v": a["peer_v"].reshape(DEPTH * EXPERTS, D),
        "g_final": a["g_final"], "ident_in": ident, "onehot_in": onehot, "maskrow_in": maskrow, "count_in": count,
        "rope_in": rope, "iota_in": iota,
    }
    nc = bacc.Bacc("TRN2", target_bir_lowering=False, num_devices=1)
    arrays, args = {}, []
    for name, v in laid.items():
        v = np.ascontiguousarray(v)
        arrays[name] = v
        args.append(nc.dram_tensor(name, list(v.shape), mybir.dt.from_np(v.dtype), kind="ExternalInput").ap())
    args.append(nc.dram_tensor("out", [TILES, P, D], F32, kind="ExternalOutput").ap())
    trunk(nc, *args)
    r = run_bass_kernel_spmd(nc, [arrays], core_ids=[0])
    return r.results[0]["out"].reshape(1, SEQ, D)
```

```python
import math
from contextlib import ExitStack

import concourse.bass as bass
from concourse import mybir

F32 = mybir.dt.float32
U32 = mybir.dt.uint32
ALU = mybir.AluOpType
ACT = mybir.ActivationFunctionType
AX = mybir.AxisListType

P = 128
D = 1024
SEQ = 256
DEPTH = 2
TILES = SEQ // P
STAGES = DEPTH * TILES
KC = D // P
A_HEADS, B_HEADS, C_HEADS, HD = 6, 4, 6, 64
A_CONFIGS = ((128, 1), (512, 4), (2048, 16))
ROPE = 32
C_QK = HD + ROPE
Q_RANK, KV_RANK = 256, 128
BUCKETS, MAX_DISTANCE = 32, 2048
BIAS_HEADS = A_HEADS + B_HEADS
EPS = 1e-6
NEG = -1e30
DISTS = 3 * P
HEADS, KEYS, TOPK = 8, 128, 16
EXPERTS = KEYS * KEYS
PICKS = HEADS * TOPK

COL_AQ, COL_AK, COL_AV = 0, 384, 768
COL_BQ, COL_BK, COL_BV = 1152, 1664, 2176
COL_C, C_WIDTH = 2688, Q_RANK + KV_RANK + ROPE
COL_GATE = 3104
GATE_CHUNKS = 6
BANK = 512

(HT0, HT1, PC, AQR, AKR, AQT, AV, AKT, BQR, BKR, BQT, BV, BKT, CT, G0, CQ0, CQ1, CKV0, CKV1, G1,
 CQT0, CQT1, CKT0, CKT1, G2, G3, G4, G5) = range(28)
GATES = (G0, G1, G2, G3, G4, G5)
YT0 = G5 + 1
BR0 = YT0 + 3
MT0 = BR0 + 6
WO0 = MT0 + 2
H2T0 = WO0 + 2
PQR0 = H2T0 + 2
PQT0 = PQR0 + 2
USES = PQT0 + 2

W_CHUNKS = ([("c", PC), ("aq", AQR), ("ak", AKR), ("av", AV), ("bq", BQR), ("bk", BKR), ("bv", BV)]
            + [(("gate", g), GATES[g]) for g in range(GATE_CHUNKS)]
            + [("wa", BR0 + 1), ("wb", BR0 + 3), ("wc", BR0 + 5), (("wo", 0), WO0), (("wo", 1), WO0 + 1),
               (("pq", 0), PQR0), (("pq", 1), PQR0 + 1)])
W_AT = {name: i for i, (name, _) in enumerate(W_CHUNKS)}
NW = len(W_CHUNKS)
W_SLOTS = 3
W_EXTRA = 2
W_WORDS = 4096


def weight_slots():
    lasting = W_AT["wc"]
    slots, fills, olds, last, turn = [], [], [], {}, 0
    for n in range(STAGES * NW):
        if n < lasting:
            slot = n % (W_SLOTS + W_EXTRA)
        elif NW <= n < NW + W_EXTRA:
            slot = W_SLOTS + n - NW
        else:
            slot, turn = turn % W_SLOTS, turn + 1
        olds.append(last.get(slot))
        last[slot] = n
        slots.append(slot)
        fills.append(slots.count(slot))
    return slots, fills, olds


W_SLOT, W_FILLS, W_OLD = weight_slots()

GROUPS = 10
FILL = (10, 14, 12, 6, 6, 2)
GATE_HALVES = (1, 2, 3, 4, 5, 6, 7, 8)
PE_HEADS = (2, 3)
PE_PICKS = len(PE_HEADS) * TOPK
LAST_HEADS = 1
DIAGS = 8
RING = 8


def kind_of(g):
    return ("A", g) if g < 3 else ("B", g - 3) if g < 7 else ("C", g - 7)


class Mark:

    def __init__(self, sem, per_stage):
        self.sem, self.per_stage = sem, per_stage

    def at(self, s, i=0):
        return s * self.per_stage + i + 1


def trunk(nc, x, rel_bias, w_in, g_mix, w_uq, g_cq, w_ukv, g_ckv, lam_vecs, g_subln, w_a, w_b, w_c, w_out, g_ffn,
          w_pq, keysT, peer_u, peer_v, g_final, ident_in, onehot_in, maskrow_in, count_in, rope_in, iota_in, out):
    table_dram = nc.dram_tensor("distance_bias", [BIAS_HEADS + 1, P, DISTS], F32, kind="Internal").ap()
    with ExitStack() as ctx:
        def sb(name, shape, dt=F32):
            return ctx.enter_context(nc.sbuf_tensor(name, shape, dt))

        def sem(name):
            return ctx.enter_context(nc.semaphore(name))

        def mark(name, per_stage):
            return Mark(sem(name), per_stage)

        rows = sb("rows", [P, RING, D])
        weights = sb("weights", [P, W_SLOTS, W_WORDS])
        ident = sb("ident", [P, P])
        bias = sb("bias", [P, BIAS_HEADS + 1, SEQ])
        count = sb("count", [P, SEQ])
        rope = sb("rope", [P, TILES, 2, 7 * 16])
        iota = sb("iota", [P, TOPK])
        headrow = sb("headrow", [BUCKETS + 2, BIAS_HEADS + 1])
        eps = sb("eps", [P, 1])
        xs = sb("xs", [P, TILES, D])
        gmix = sb("gmix", [P, D])
        gffn = sb("gffn", [P, D])
        gcq = sb("gcq", [P, Q_RANK])
        gckv = sb("gckv", [P, KV_RANK])
        gsub = sb("gsub", [P, P])
        lams = sb("lams", [P, DEPTH, 2])
        neglam = sb("neglam", [P, DEPTH])
        wuq = sb("wuq", [P, 2, C_HEADS * C_QK])
        wukv = sb("wukv", [P, C_HEADS * P])
        keys = sb("keys", [P, HEADS, KEYS])
        hrow = sb("hrow", [P, D])
        hT = sb("hT", [P, KC, P])
        h2row = sb("h2row", [P, D])
        stat = sb("stat", [P, 16])
        qTA = sb("qTA", [P, 3, P])
        kTA = sb("kTA", [P, 3, SEQ])
        vA = sb("vA", [P, TILES, A_HEADS * HD])
        qTB = sb("qTB", [P, B_HEADS, P])
        kTB = sb("kTB", [P, B_HEADS, SEQ])
        vB = sb("vB", [P, TILES, B_HEADS * 2 * HD])
        krot = sb("krot", [P, ROPE])
        qTC = sb("qTC", [C_QK, C_HEADS, P])
        kTC = sb("kTC", [C_QK, C_HEADS, SEQ])
        vC = sb("vC", [P, TILES, C_HEADS * HD])
        attention = sb("attention", [P, 3, 2 * 2 * SEQ])
        negmax = sb("negmax", [P, 2, 2])

        denom = sb("denom", [P, 2, 2])
        recip = sb("recip", [P, 2, 2])
        lamr = sb("lamr", [P, 1])

        mixers = sb("mixers", [P, 2 * 10 * P])
        gates = sb("gates", [P, GATE_CHUNKS * BANK])
        tops = sb("tops", [P, HEADS * 2, TOPK])
        topi = sb("topi", [P, HEADS * 2, TOPK], U32)
        best = sb("best", [P, HEADS, TOPK])
        bestpos = sb("bestpos", [P, HEADS, TOPK], U32)
        gsum = sb("gsum", [P, 2, HEADS])
        pickw = sb("pickw", [P, 2, PICKS])
        index = sb("index", [P, 2, PICKS], U32)
        indexh = sb("indexh", [P, 2, TOPK], U32)
        acts = sb("acts", [P, PICKS])
        coef = sb("coef", [P, PICKS])

        y = mixers[:, 0:10 * P]
        yT = mixers[:, 10 * P:20 * P].rearrange("p (b t) -> p b t", b=10)
        logits = attention[:, 0, :].rearrange("p (b m n) -> p b m n", b=2, m=2)
        probsT = attention[:, 1, :].rearrange("p (b n) -> p b n", b=2)
        probs = attention[:, 2, :].rearrange("p (b m n) -> p b m n", b=2, m=2)
        scores = attention[:, 0:2, :].rearrange("p a (j k) -> p (a j) k", k=KEYS)
        pqT = attention[:, 2, :].rearrange("p (h t) -> p h t", h=HEADS)
        diags = attention[:, 2, :].rearrange("p (d t) -> p d t", d=DIAGS)
        onehot = gates[0:BUCKETS + 2, 0:BANK]
        table = gates[0:BIAS_HEADS + 1, BANK:2 * BANK]
        lam_at = 2 * BANK
        lamv = gates[:, lam_at:lam_at + BANK].rearrange("p (l v d) -> p l v d", l=DEPTH, v=4)

        crow = mixers[:, 0:C_WIDTH]
        at = C_WIDTH
        cnorm, at = mixers[:, at:at + Q_RANK + KV_RANK], at + Q_RANK + KV_RANK
        cT, at = mixers[:, at:at + 3 * P], at + 3 * P
        rowtmp = mixers[:, at:at + 2 * BANK].rearrange("p (b n) -> p b n", b=2)
        assert at + 2 * BANK <= 20 * P
        at = GATE_CHUNKS * BANK - 2 * C_HEADS * C_QK - 4 * 7 * 16
        assert at >= 2 * BANK
        qrow, at = gates[:, at:at + C_HEADS * C_QK], at + C_HEADS * C_QK
        krow, at = gates[:, at:at + C_HEADS * C_QK], at + C_HEADS * C_QK
        rot = gates[:, at:at + 4 * 7 * 16]
        cT = cT.rearrange("p (c t) -> p c t", c=3)
        qrow, krow = (z.rearrange("p (h c) -> p h c", h=C_HEADS) for z in (qrow, krow))
        rot = rot.rearrange("p (j n) -> p j n", j=4)
        cand = gates[:, 0:PICKS * TOPK]
        at = PICKS * TOPK
        topf, at = gates[:, at:at + HEADS * 2 * TOPK].rearrange("p (j k) -> p j k", k=TOPK), at + HEADS * 2 * TOPK
        pos, at = gates[:, at:at + 2 * PICKS].bitcast(U32).rearrange("p (j k) -> p j k", j=2), at + 2 * PICKS
        posf, at = gates[:, at:at + 2 * PICKS].rearrange("p (j k) -> p j k", j=2), at + 2 * PICKS
        part, at = gates[:, at:at + 2 * PICKS].rearrange("p (j k) -> p j k", j=2), at + 2 * PICKS
        mix = hrow
        tmp = attention[:, 0, :].rearrange("p (b n) -> p b n", b=2)
        tmp = [tmp[:, half, :] for half in range(2)]

        def ps(name, words):
            return ctx.enter_context(nc.psum_tensor(name, [P, words], F32))

        proj = [ps(f"proj{i}", BANK) for i in range(2)]
        sc = [ps(f"sc{i}", 2 * BANK) for i in range(2)]
        psT = ps("psT", BANK)
        psO = ps("psO", BANK)
        vsum = (psT, psO)

        x_in, ident_sem, consts_in, table_out, bias_in = (sem(n) for n in (
            "x_in", "ident_in", "consts_in", "table_out", "bias_in"))
        lam_in, head_in = sem("lam_in"), sem("head_in")
        mix_params = sem("mix_params")
        ffn_params = sem("ffn_params")
        gmix_in = sem("gmix_in")
        w_in_sem = [sem(f"w_in{i}") for i in range(W_SLOTS + W_EXTRA)]
        row_in = [sem(f"row_in{i}") for i in range(RING)]
        headrow_zero, table_ps, table_sb, eps_set = (sem(n) for n in (
            "headrow_zero", "table_ps", "table_sb", "eps_set"))
        lam_sums, lam_exps = sem("lam_sums"), sem("lam_exps")
        proj_ready = mark("proj_ready", USES)
        proj_free = [sem("proj_free0"), sem("proj_free1")]
        h_ready = mark("h_ready", 1)
        mean_ready = mark("mean_ready", 4)
        root_ready = mark("root_ready", 4)
        cnorm_ready = mark("cnorm_ready", 1)
        qrope_ready = mark("qrope_ready", 1)
        krope_ready = mark("krope_ready", 1)
        s_ready = mark("s_ready", GROUPS)
        neg_ready = mark("neg_ready", GROUPS)
        e_ready = mark("e_ready", GROUPS)
        p_ready = mark("p_ready", GROUPS)
        pT_ready = mark("pT_ready", GROUPS)
        pTs_ready = mark("pTs_ready", GROUPS)
        o_ready = mark("o_ready", GROUPS)
        o_used = mark("o_used", GROUPS)
        y_ready = mark("y_ready", 1)
        sig_ready = mark("sig_ready", 1)
        mix_ready = mark("mix_ready", 2)
        h2_ready = mark("h2_ready", 1)
        route_ready = mark("route_ready", 2)
        best_ready = mark("best_ready", 1)
        bexp_ready = mark("bexp_ready", 1)
        index_ready = mark("index_ready", 2)

        index_copied = sem("index_copied")

        rows_used = sem("rows_used")
        pe_rows_used = sem("pe_rows_used")
        diag_ready = sem("diag_ready")
        pe_sum_used = sem("pe_sum_used")
        pool_steps = sem("pool_steps")
        gelu_ready = mark("gelu_ready", 1)
        coef_ready = mark("coef_ready", 1)
        fin_mean, fin_root, fin_row = sem("fin_mean"), sem("fin_root"), sem("fin_row")
        out_written = sem("out_written")
        dve_done = sem("dve_done")

        def bank_of(s, use):
            return (s * USES + use) % 2

        def freed(s, use):
            return (s * USES + use) // 2 + 1

        def w_slot(s, name, kc, width):
            slot = W_SLOT[s * NW + W_AT[name]]
            if slot < W_SLOTS:
                whole = weights[:, slot, :]
            else:
                n = W_WORDS // D
                whole = rows[:, (slot - W_SLOTS) * n:(slot - W_SLOTS + 1) * n, :].rearrange("p r d -> p (r d)")
            return whole[:, 0:kc * width].rearrange("p (c n) -> p c n", c=kc)

        def row_step(s, phase, k):
            return (s * 2 + phase) * PICKS + k

        def dve_rows(s, phase, head):
            past = phase * PICKS + head * TOPK
            return s * (2 * PICKS - PE_PICKS) + past - (PE_PICKS if phase and head > PE_HEADS[-1] else 0)

        def pe_rows(s, head):
            return s * PE_PICKS + (head - PE_HEADS[0]) * TOPK

        block = ctx.enter_context(nc.Block())

        @block.sync
        def _(sp):
            def bcast(vec):
                return vec.partition_broadcast(P)

            def load_mix_params(l):
                for dst, src in ((gcq[:, :], bcast(g_cq[l])),
                                 (gckv[:, :], bcast(g_ckv[l])), (gsub[:, :], bcast(g_subln[l])),
                                 (wuq[:, :, :], w_uq[l].rearrange("(c p) n -> p c n", p=P)), (wukv[:, :], w_ukv[l])):
                    sp.dma_start(dst, src).then_inc(mix_params, 16)

            def load_ffn_params(l):
                sp.dma_start(gffn[:, :], bcast(g_ffn[l])).then_inc(ffn_params, 16)
                sp.dma_start(keys[:, :, :], keysT[l].rearrange("p (h k) -> p h k", h=HEADS)).then_inc(ffn_params, 16)

            def source(l, name):
                cols = {"c": (COL_C, C_WIDTH), "aq": (COL_AQ, 384), "ak": (COL_AK, 384), "av": (COL_AV, 384),
                        "bq": (COL_BQ, 512), "bk": (COL_BK, 512), "bv": (COL_BV, 512)}
                if name in ("wa", "wb", "wc"):
                    w = {"wa": w_a, "wb": w_b, "wc": w_c}[name]
                    return w[l].rearrange("(c p) n -> p c n", p=P)
                if name in cols:
                    at, n = cols[name]
                    w = w_in
                else:
                    kind, i = name
                    w, at = {"gate": (w_in, COL_GATE), "wo": (w_out, 0), "pq": (w_pq, 0)}[kind]
                    at, n = at + i * BANK, BANK
                return w[l].rearrange("(c p) n -> p c n", p=P)[:, :, at:at + n]

            def load_weights(s, name):
                n = s * NW + W_AT[name]
                old = W_OLD[n]
                if old is not None:
                    sp.wait_ge(proj_ready.sem, proj_ready.at(old // NW, W_CHUNKS[old % NW][1]))
                src = source(s // TILES, name)
                sp.dma_start(w_slot(s, name, src.shape[1], src.shape[2]), src).then_inc(w_in_sem[W_SLOT[n]], 16)

            sp.dma_start(xs[:, 0, :], x[0]).then_inc(x_in, 16)
            sp.dma_start(ident[:, :], ident_in).then_inc(ident_sem, 16)
            sp.dma_start(gmix[:, :], bcast(g_mix[0])).then_inc(gmix_in, 16)
            load_weights(0, "c")
            load_weights(0, "aq")
            sp.wait_ge(headrow_zero, 1)
            sp.dma_start(headrow[0:BUCKETS, 0:BIAS_HEADS], rel_bias).then_inc(head_in, 16)
            sp.dma_start(headrow[BUCKETS:BUCKETS + 2, :], maskrow_in).then_inc(head_in, 16)
            sp.dma_start(onehot, onehot_in).then_inc(head_in, 16)
            load_weights(0, "ak")
            sp.dma_start(gates[:, lam_at:lam_at + BANK], bcast(lam_vecs)).then_inc(lam_in, 16)
            load_weights(0, "av")
            load_weights(0, "bq")
            load_mix_params(0)
            load_weights(0, "bk")
            sp.dma_start(rope[:, :, :, :], rope_in.rearrange("(t p) a n -> p t a n", p=P)).then_inc(consts_in, 16)
            sp.dma_start(count[:, :], count_in).then_inc(consts_in, 16)
            sp.dma_start(iota[:, :], iota_in).then_inc(consts_in, 16)
            load_weights(0, "bv")
            sp.wait_ge(table_sb, 1)
            sp.dma_start(table_dram, table[:, 0:DISTS].unsqueeze(1).to_broadcast([BIAS_HEADS + 1, P, DISTS])).then_inc(table_out, 16)
            load_weights(0, ('gate', 0))
            sp.wait_ge(table_out, 16)
            sp.dma_start(bias[:, :, :], bass.AP(tensor=table_dram.tensor, offset=P - 1,
                                                ap=[[DISTS - 1, P], [P * DISTS, BIAS_HEADS + 1], [1, SEQ]])).then_inc(bias_in, 16)
            load_weights(0, ('gate', 1))
            load_ffn_params(0)
            sp.dma_start(xs[:, 1, :], x[1]).then_inc(x_in, 16)
            for s in range(STAGES):
                if s == TILES:
                    sp.wait_ge(y_ready.sem, y_ready.at(s - 1))
                    sp.dma_start(gmix[:, :], bcast(g_mix[1])).then_inc(gmix_in, 16)
                    load_mix_params(1)
                for name, _ in W_CHUNKS[(9 if s == 0 else 0):]:
                    if s == TILES and name == ("gate", 0):
                        sp.wait_ge(route_ready.sem, route_ready.at(s - 1, 1))
                        sp.wait_ge(h2_ready.sem, h2_ready.at(s - 1))
                        load_ffn_params(1)
                    load_weights(s, name)
            sp.wait_ge(h_ready.sem, h_ready.at(STAGES - 1))
            sp.dma_start(gmix[:, :], bcast(g_final)).then_inc(gmix_in, 16)
            for t in range(TILES):
                sp.wait_ge(fin_row, t + 1)
                sp.dma_start(out[t], (hrow if t == 0 else h2row)[:, :]).then_inc(out_written, 16)
            sp.wait_ge(out_written, 16 * TILES)

        @block.gpsimd
        def _(pool):
            def consumed(s, phase, head, n):
                if isinstance(head, int):
                    if head < 0:
                        s, phase, head = (s, 0, head + HEADS) if phase else (s - 1, 1, head + HEADS)
                    if phase and head in PE_HEADS:
                        pool.wait_ge(pe_rows_used, pe_rows(s, head) + n)
                        return
                    pool.wait_ge(rows_used, dve_rows(s, phase, head) + n)
                    return
                pool.wait_ge(rows_used, head * TOPK + (dve_rows(s, phase, 0) + n))
                pool.sem_inc(pool_steps, 1)

            def gather_head(s, phase, head, odd):
                known = isinstance(head, int)
                number = head + (s * 2 + phase) * HEADS
                if not known or number >= 2:
                    consumed(s, phase, head - 2, TOPK)
                nc.gpsimd.tensor_copy(indexh[:, odd, :], index[:, s % 2, bass.ds(head * TOPK, TOPK)])\
                    .then_inc(index_copied, 1)
                pool.wait_ge(index_copied, number + 1)
                if not known:
                    pool.sem_inc(pool_steps, 1)
                for k in range(TOPK):
                    if k >= RING:
                        consumed(s, phase, head, k + 1 - RING)
                    elif not known or number > 0:
                        consumed(s, phase, head - 1, k + 1 + TOPK - RING)
                    pool.indirect_dma_start(rows[:, k % RING, :], None, (peer_u, peer_v)[phase],
                                            bass.IndirectOffsetOnAxis(ap=indexh[:, odd, k:k + 1], axis=0))\
                        .then_inc(row_in[k % RING], 16)

            def gather_pairs(s, phase, first, end):
                with pool.Fori(first, end) as pair:
                    for odd in range(2):
                        gather_head(s, phase, pair * 2 + odd, odd)

            pool.wait_ge(proj_ready.sem, proj_ready.at(1, W_CHUNKS[W_EXTRA - 1][1]))
            for s in range(STAGES):
                pool.wait_ge(index_ready.sem, index_ready.at(s, 0))
                for h in range(2):
                    gather_head(s, 0, h, h)
                gather_pairs(s, 0, 1, HEADS // 4)
                pool.wait_ge(index_ready.sem, index_ready.at(s, 1))
                gather_pairs(s, 0, HEADS // 4, HEADS // 2)
                for h in range(PE_HEADS[-1] + 3):
                    gather_head(s, 1, h, h % 2)
                gather_pairs(s, 1, (PE_HEADS[-1] + 3) // 2, HEADS // 2)

        @block.scalar
        def _(act):
            def copy(dst, src, scale=1.0):
                return nc.scalar.activation(dst, src, ACT.Copy, scale=scale)

            def evac(s, use, dst, src=None, scale=1.0):
                b = bank_of(s, use)
                act.wait_ge(proj_ready.sem, proj_ready.at(s, use))
                src = proj[b][:, 0:dst.free_size()] if src is None else src(proj[b])
                if len(dst.shape) == 3 and len(src.shape) == 2:
                    src = src.rearrange("p (a b) -> p a b", a=dst.shape[1])
                copy(dst, src, scale).then_inc(proj_free[b], 1)

            def root(s, i, n):
                act.wait_ge(mean_ready.sem, mean_ready.at(s, i))
                nc.scalar.activation(stat[:, 4:4 + n], stat[:, 0:n], ACT.Sqrt, bias=eps[:, 0:1])\
                    .then_inc(root_ready.sem, 1)

            def dense_first(s):
                t = s % TILES
                now = slice(t * P, (t + 1) * P)
                root(s, 0, 1)
                for i in range(2):
                    evac(s, HT0 + i, hT[:, 4 * i:4 * i + 4, :])
                evac(s, PC, crow)
                if s == 0:
                    tables()
                evac(s, AQR, rowtmp[:, 0, 0:A_HEADS * HD])
                evac(s, AKR, rowtmp[:, 1, 0:A_HEADS * HD])
                evac(s, AQT, qTA[:, :, :], scale=HD ** -0.5)
                evac(s, AV, vA[:, t, :])
                evac(s, AKT, kTA[:, :, now])
                evac(s, BQR, rowtmp[:, 0, :])
                evac(s, BKR, rowtmp[:, 1, :])
                evac(s, BQT, qTB[:, :, :], scale=HD ** -0.5)
                evac(s, BV, vB[:, t, :])
                evac(s, BKT, kTB[:, :, now])
                if s > 0:
                    picks_exp(s - 1)
                root(s, 1, 2)
                evac(s, CT, cT[:, :, :])
                evac(s, G0, gates[:, 0:BANK])
                for i in range(2):
                    evac(s, CQ0 + i, qrow[:, 3 * i:3 * i + 3, :], scale=C_QK ** -0.5)
                for i in range(2):
                    b = bank_of(s, CKV0 + i)
                    act.wait_ge(proj_ready.sem, proj_ready.at(s, CKV0 + i))
                    src = proj[b][:, 0:3 * P].rearrange("p (h c) -> p h c", h=3)
                    copy(krow[:, 3 * i:3 * i + 3, 0:HD], src[:, :, 0:HD])
                    copy(vC[:, t, 3 * i * HD:3 * (i + 1) * HD].rearrange("p (h c) -> p h c", h=3), src[:, :, HD:P])\
                        .then_inc(proj_free[b], 1)
                evac(s, G1, gates[:, BANK:2 * BANK])
                for i, (h0, h1) in enumerate(((0, 4), (4, 6))):
                    evac(s, CQT0 + i, qTC[:, h0:h1, :], src=lambda pb, n=(h1 - h0) * P: pb[0:C_QK, 0:n])
                for i, (h0, h1) in enumerate(((0, 4), (4, 6))):
                    evac(s, CKT0 + i, kTC[:, h0:h1, now], src=lambda pb, n=(h1 - h0) * P: pb[0:C_QK, 0:n])

                nk = (t + 1) * P
                for i in range(GROUPS + 2):
                    if i < GROUPS:
                        exps(s, i, nk)
                    if i in GATE_HALVES and GATE_HALVES.index(i) % 2 == 1:
                        g = 2 + GATE_HALVES.index(i) // 2
                        evac(s, GATES[g], gates[:, g * BANK:(g + 1) * BANK])
                    if 0 <= i - 1 < GROUPS:
                        transposed(s, i - 1, nk)
                root(s, 2, 4)

            def exps(s, g, nk):
                b = g % 2
                act.wait_ge(neg_ready.sem, neg_ready.at(s, g))
                if g >= 2:
                    act.wait_ge(pT_ready.sem, pT_ready.at(s, g - 2))
                for m in range(2):
                    acc = {} if kind_of(g)[0] == "A" else {"accum_out": denom[:, b, m:m + 1]}
                    last = nc.scalar.activation(probs[:, b, m, 0:nk], logits[:, b, m, 0:nk], ACT.Exp,
                                                bias=negmax[:, b, m:m + 1], **acc)
                last.then_inc(e_ready.sem, 1)

            def transposed(s, g, nk):
                n = nk if kind_of(g)[0] == "B" else 2 * nk
                act.wait_ge(pT_ready.sem, pT_ready.at(s, g))
                if g >= 2:
                    act.wait_ge(o_ready.sem, o_ready.at(s, g - 2))
                copy(probsT[:, g % 2, 0:n], psT[:, 0:n]).then_inc(pTs_ready.sem, 1)

            def diagonals(s):
                act.wait_ge(coef_ready.sem, coef_ready.at(s))
                for j in range(PE_PICKS):
                    n = s * PE_PICKS + j
                    if j >= DIAGS:
                        act.wait_ge(pe_rows_used, n - DIAGS + 1)
                    k = PE_HEADS[0] * TOPK + j
                    copy(diags[:, j % DIAGS, :], ident[:, :], scale=coef[:, k:k + 1]).then_inc(diag_ready, 1)

            def gelu(s):
                act.wait_ge(rows_used, dve_rows(s, 1, 0))
                nc.scalar.activation(coef[:, :], acts[:, :], ACT.Gelu).then_inc(gelu_ready.sem, 1)

            def picks_exp(s):
                act.wait_ge(best_ready.sem, best_ready.at(s))
                nc.scalar.activation(pickw[:, s % 2, :], pickw[:, s % 2, :], ACT.Exp).then_inc(bexp_ready.sem, 1)

            def tables():
                act.wait_ge(table_ps, 1)
                copy(table, psO[0:BIAS_HEADS + 1, :]).then_inc(table_sb, 1)
                act.wait_ge(lam_sums, 1)
                nc.scalar.activation(lams[:, :, :], lams[:, :, :], ACT.Exp).then_inc(lam_exps, 1)

            def dense_second(s):
                for g in (G4, G5):
                    act.wait_ge(proj_free[bank_of(s, g)], freed(s, g))
                nc.scalar.activation(gates[:, :], gates[:, :], ACT.Sigmoid).then_inc(sig_ready.sem, 1)
                for i, (b0, b1) in enumerate(((0, 4), (4, 8), (8, 10))):
                    evac(s, YT0 + i, yT[:, b0:b1, :])
                for i in range(2):
                    evac(s, MT0 + i, hT[:, 4 * i:4 * i + 4, :])
                root(s, 3, 1)
                for i in range(2):
                    evac(s, H2T0 + i, hT[:, 4 * i:4 * i + 4, :])
                if s > 0:
                    gelu(s - 1)
                for i in range(2):
                    evac(s, PQR0 + i, rowtmp[:, i, :])
                for i in range(2):
                    evac(s, PQT0 + i, pqT[:, 4 * i:4 * i + 4, :])
                if s > 0:
                    act.wait_ge(route_ready.sem, route_ready.at(s, 1))
                    diagonals(s - 1)

            act.wait_ge(eps_set, 1)
            for s in range(STAGES):
                dense_first(s)
                dense_second(s)
            picks_exp(STAGES - 1)
            for t in range(TILES):
                if t == TILES - 1:
                    gelu(STAGES - 1)
                    diagonals(STAGES - 1)
                    nc.scalar.activation(stat[:, 12:13], eps[:, 0:1], ACT.Sqrt)
                act.wait_ge(fin_mean, t + 1)
                nc.scalar.activation(stat[:, 4:5], stat[:, 0:1], ACT.Sqrt, bias=eps[:, 0:1]).then_inc(fin_root, 1)

        @block.vector
        def _(dve):
            done = [0]

            def noted(ins):
                done[0] += 1
                return ins.then_inc(dve_done, 1)

            def settle():
                dve.wait_ge(dve_done, done[0])

            def link(ins):
                noted(ins)
                settle()

            V = nc.vector

            def mean_square(dst, src, junk, n):
                return V.scalar_tensor_tensor(out=junk, in0=src, scalar=1.0 / n, in1=src, op0=ALU.mult, op1=ALU.mult,
                                              accum_out=dst)

            def dot_step(s, slot, k, n):
                V.scalar_tensor_tensor(out=rows[:, slot, :], in0=rows[:, slot, :], scalar=1.0, in1=h2row[:, :],
                                       op0=ALU.mult, op1=ALU.mult, accum_out=acts[:, bass.ds(k, 1)])\
                    .then_inc(rows_used, 1)

            def add_step(s, slot, k, n):
                dve.wait_ge(rows_used, n)
                t = s % TILES
                V.scalar_tensor_tensor(out=xs[:, t, :], in0=rows[:, slot, :], scalar=coef[:, bass.ds(k, 1)],
                                       in1=xs[:, t, :], op0=ALU.mult, op1=ALU.add).then_inc(rows_used, 1)

            class Retrieval:

                def __init__(self, s, phase):
                    self.s, self.phase, self.k = s, phase, 0

                def head(self, h, slots=range(TOPK)):
                    step = (dot_step, add_step)[self.phase]
                    skipped = PE_HEADS[0] <= self.k // TOPK and self.phase
                    for k in slots:
                        fills = h * (TOPK // RING) + (row_step(self.s, self.phase, k) // RING + 1)
                        dve.wait_ge(row_in[k % RING], fills * 16)
                        before = dve_rows(self.s, self.phase, 0) + k - (PE_PICKS if skipped else 0)
                        step(self.s, k % RING, h * TOPK + k, h * TOPK + before)

                def part(self, n):
                    n = min(n, PICKS - self.k)
                    while n > 0:
                        h, at = divmod(self.k, TOPK)
                        m = min(n, TOPK - at)
                        self.head(h, range(at, at + m))
                        self.k, n = self.k + m, n - m

                def heads(self, n):
                    h = self.k // TOPK
                    assert self.k % TOPK == 0
                    if n > 0:
                        with dve.Fori(h, h + n) as i:
                            self.head(i)
                        self.k += n * TOPK

                def rest(self):
                    self.part(-self.k % TOPK)
                    self.heads((PICKS - self.k) // TOPK)

                def over(self):
                    self.k = (PE_HEADS[-1] + 1) * TOPK

                def pe_sum(self):
                    t = self.s % TILES
                    dve.wait_ge(rows_used, dve_rows(self.s, 1, self.k // TOPK))
                    dve.wait_ge(pe_rows_used, pe_rows(self.s, PE_HEADS[-1] + 1))
                    for half in range(2):
                        xh = xs[:, t, half * BANK:(half + 1) * BANK]
                        V.tensor_tensor(xh, vsum[half][:, :], xh, ALU.add).then_inc(pe_sum_used, 1)
                    dve.wait_ge(pe_sum_used, 2 * (self.s + 1))

            class Nothing:
                def part(self, n):
                    pass

                def rest(self):
                    pass

            def coefficients(s):
                dve.wait_ge(gelu_ready.sem, gelu_ready.at(s))
                V.tensor_tensor(coef[:, :], coef[:, :], pickw[:, s % 2, :], ALU.mult).then_inc(coef_ready.sem, 1)
                dve.wait_ge(coef_ready.sem, coef_ready.at(s))

            def first_norm(s):
                l, t = divmod(s, TILES)
                if s < TILES:
                    dve.wait_ge(x_in, 16 * (t + 1))
                else:
                    dve.wait_ge(rows_used, dve_rows(s - TILES + 1, 0, 0))
                mean_square(stat[:, 0:1], xs[:, t, :], hrow[:, :], D).then_inc(mean_ready.sem, 1)
                if t == 0:
                    dve.wait_ge(gmix_in, 16 * (l + 1))
                dve.wait_ge(root_ready.sem, root_ready.at(s, 0))
                link(V.reciprocal(stat[:, 8:9], stat[:, 4:5]))
                V.scalar_tensor_tensor(out=hrow[:, :], in0=xs[:, t, :], scalar=stat[:, 8:9], in1=gmix[:, :],
                                       op0=ALU.mult, op1=ALU.mult).then_inc(h_ready.sem, 1)

            def lambdas():
                dve.wait_ge(lam_in, 16)
                for l in range(DEPTH):
                    for j in range(2):
                        junk = (2 * l + j) * HD
                        last = V.scalar_tensor_tensor(out=tmp[0][:, junk:junk + HD], in0=lamv[:, l, 2 * j, :], scalar=1.0,
                                                      in1=lamv[:, l, 2 * j + 1, :], op0=ALU.mult, op1=ALU.mult,
                                                      accum_out=lams[:, l, j:j + 1])
                last.then_inc(lam_sums, 1)
                dve.wait_ge(lam_exps, 1)
                for l in range(DEPTH):
                    link(V.tensor_tensor(neglam[:, l:l + 1], lams[:, l, 1:2], lams[:, l, 0:1], ALU.subtract))
                    link(V.tensor_scalar(neglam[:, l:l + 1], neglam[:, l:l + 1],
                                         -(0.8 - 0.6 * math.exp(-0.3 * l)), None, ALU.add))

            def dense_first(s, fill):
                l, t = divmod(s, TILES)
                nk = (t + 1) * P
                if s != 1:
                    first_norm(s)
                if s == 0:
                    lambdas()
                if t == 0:
                    dve.wait_ge(mix_params, 80 * (l + 1))
                    lam_init = 0.8 - 0.6 * math.exp(-0.3 * l)
                    link(V.tensor_scalar(gsub[:, :], gsub[:, :], 1.0 - lam_init, None, ALU.mult))
                fill.part(FILL[0])
                dve.wait_ge(proj_free[bank_of(s, PC)], freed(s, PC))
                mean_square(stat[:, 0:1], crow[:, 0:Q_RANK], cnorm[:, 0:Q_RANK], Q_RANK)
                mean_square(stat[:, 1:2], crow[:, Q_RANK:Q_RANK + KV_RANK], cnorm[:, Q_RANK:], KV_RANK)\
                    .then_inc(mean_ready.sem, 1)
                dve.wait_ge(root_ready.sem, root_ready.at(s, 1))
                link(V.reciprocal(stat[:, 8:10], stat[:, 4:6]))
                V.scalar_tensor_tensor(out=cnorm[:, 0:Q_RANK], in0=crow[:, 0:Q_RANK], scalar=stat[:, 8:9],
                                       in1=gcq[:, :], op0=ALU.mult, op1=ALU.mult)
                V.scalar_tensor_tensor(out=cnorm[:, Q_RANK:], in0=crow[:, Q_RANK:Q_RANK + KV_RANK],
                                       scalar=stat[:, 9:10], in1=gckv[:, :], op0=ALU.mult, op1=ALU.mult)\
                    .then_inc(cnorm_ready.sem, 1)
                fill.part(FILL[1])
                if s > 0:
                    picks_softmax(s - 1)

                if s == 0:
                    dve.wait_ge(consts_in, 48)

                def rotate(x1, x2, o1, o2, heads):
                    n = heads * 16
                    r = [rot[:, j, 0:n].rearrange("p (h c) -> p h c", h=heads) for j in range(4)]
                    cos, sin = (rope[:, t, j, 0:n].rearrange("p (h c) -> p h c", h=heads) for j in range(2))
                    for dst, a, f in ((r[0], x1, cos), (r[1], x2, sin), (r[2], x1, sin), (r[3], x2, cos)):
                        noted(V.tensor_tensor(dst, a, f, ALU.mult))
                    settle()
                    noted(V.tensor_tensor(o1, r[0], r[1], ALU.subtract))
                    return V.tensor_tensor(o2, r[2], r[3], ALU.add)

                c0 = Q_RANK + KV_RANK
                one = lambda ap: ap.rearrange("p (h c) -> p h c", h=1)
                link(rotate(one(crow[:, c0:c0 + 16]), one(crow[:, c0 + 16:c0 + 32]),
                            one(krot[:, 0:16]), one(krot[:, 16:32]), 1))
                V.tensor_copy(krow[:, :, HD:C_QK], krot[:, :].unsqueeze(1).to_broadcast([P, C_HEADS, ROPE]))\
                    .then_inc(krope_ready.sem, 1)
                for i in range(2):
                    dve.wait_ge(proj_free[bank_of(s, CQ0 + i)], freed(s, CQ0 + i))
                q1, q2 = qrow[:, :, HD:HD + 16], qrow[:, :, HD + 16:C_QK]
                rotate(q1, q2, q1, q2, C_HEADS).then_inc(qrope_ready.sem, 1)
                fill.part(FILL[2])

                for i in range(GROUPS + 2):
                    if i < GROUPS:
                        masked(s, i, t, nk)
                    if 0 <= i - 1 < GROUPS:
                        weigh(s, i - 1, l, nk)
                    if 0 <= i - 2 < GROUPS:
                        outputs(s, i - 2)
                    if i - 2 == 6:
                        dve.wait_ge(o_used.sem, o_used.at(s, 6))
                        for h in range(B_HEADS):
                            last = mean_square(stat[:, h:h + 1], y[:, (3 + h) * P:(4 + h) * P], mixers[:, (10 + h) * P:(11 + h) * P], P)
                        last.then_inc(mean_ready.sem, 1)
                    fill.part(FILL[3])
                dve.wait_ge(root_ready.sem, root_ready.at(s, 2))
                link(V.reciprocal(stat[:, 8:12], stat[:, 4:8]))
                for h in range(B_HEADS):
                    yh = y[:, (3 + h) * P:(4 + h) * P]
                    last = V.scalar_tensor_tensor(out=yh, in0=yh, scalar=stat[:, 8 + h:9 + h], in1=gsub[:, :],
                                                  op0=ALU.mult, op1=ALU.mult)
                last.then_inc(y_ready.sem, 1)

            def masked(s, g, t, nk):
                b, (kind, j) = g % 2, kind_of(g)
                first = P * (TILES - 1 - t)
                if s == 0 and g == 0:
                    dve.wait_ge(bias_in, 16)
                if kind == "A":
                    add = bias[:, 2 * j:2 * j + 2, first:first + nk]
                else:
                    row = A_HEADS + j if kind == "B" else BIAS_HEADS
                    add = bias[:, row, first:first + nk].unsqueeze(1).to_broadcast([P, 2, nk])
                dve.wait_ge(s_ready.sem, s_ready.at(s, g))
                if g >= 2:
                    dve.wait_ge(e_ready.sem, e_ready.at(s, g - 2))
                raw = sc[b][:, :].rearrange("p (m n) -> p m n", m=2)[:, :, 0:nk]
                link(V.tensor_tensor(logits[:, b, :, 0:nk], raw, add, ALU.add))
                V.tensor_reduce(negmax[:, b, :], logits[:, b, :, 0:nk], AX.X, ALU.max, negate=True)\
                    .then_inc(neg_ready.sem, 1)

            def weigh(s, g, l, nk):
                b, (kind, _) = g % 2, kind_of(g)
                dve.wait_ge(e_ready.sem, e_ready.at(s, g))
                if g >= 2:
                    dve.wait_ge(o_used.sem, o_used.at(s, g - 2))
                if kind == "A":
                    first = SEQ - nk
                    for m in range(2):
                        last = V.scalar_tensor_tensor(out=probs[:, b, m, 0:nk], in0=probs[:, b, m, 0:nk], scalar=1.0,
                                                      in1=count[:, first:first + nk], op0=ALU.mult, op1=ALU.mult,
                                                      accum_out=denom[:, b, m:m + 1])
                    link(last)
                    V.reciprocal(recip[:, b, :], denom[:, b, :]).then_inc(p_ready.sem, 1)
                elif kind == "B":
                    link(V.reciprocal(recip[:, b, :], denom[:, b, :]))
                    link(V.scalar_tensor_tensor(out=lamr[:, :], in0=denom[:, b, 0:1], scalar=recip[:, b, 1:2],
                                                in1=neglam[:, l:l + 1], op0=ALU.mult, op1=ALU.mult))
                    V.scalar_tensor_tensor(out=probs[:, b, 0, 0:nk], in0=probs[:, b, 1, 0:nk], scalar=lamr[:, 0:1],
                                           in1=probs[:, b, 0, 0:nk], op0=ALU.mult, op1=ALU.add)\
                        .then_inc(p_ready.sem, 1)
                else:
                    V.reciprocal(recip[:, b, :], denom[:, b, :]).then_inc(p_ready.sem, 1)

            def outputs(s, g):
                b, (kind, _) = g % 2, kind_of(g)
                dve.wait_ge(o_ready.sem, o_ready.at(s, g))
                dst = y[:, g * P:(g + 1) * P]
                if kind == "B":
                    V.tensor_scalar(dst, psO[:, 0:P], recip[:, b, 0:1], None, ALU.mult).then_inc(o_used.sem, 1)
                else:
                    V.tensor_tensor(dst.rearrange("p (m c) -> p m c", m=2),
                                    psO[:, 0:P].rearrange("p (m c) -> p m c", m=2),
                                    recip[:, b, :].unsqueeze(2).to_broadcast([P, 2, HD]), ALU.mult)\
                        .then_inc(o_used.sem, 1)

            def dense_second(s, dots, adds):
                l, t = divmod(s, TILES)
                dve.wait_ge(sig_ready.sem, sig_ready.at(s))
                dots.part(FILL[4])
                for br in range(3):
                    for half in range(2):
                        cols = slice(half * BANK, (half + 1) * BANK)
                        use = BR0 + 2 * br + half
                        b = bank_of(s, use)
                        gate = gates[:, br * D + half * BANK:br * D + (half + 1) * BANK]
                        dve.wait_ge(proj_ready.sem, proj_ready.at(s, use))
                        V.tensor_tensor(mix[:, cols] if br == 0 else tmp[half], proj[b][:, :], gate, ALU.mult)\
                            .then_inc(proj_free[b], 1)
                        dve.wait_ge(proj_free[b], freed(s, use))
                        if br > 0:
                            add = V.tensor_tensor(mix[:, cols], mix[:, cols], tmp[half], ALU.add)
                            if br == 2:
                                add.then_inc(mix_ready.sem, 1)
                            else:
                                noted(add)
                        dots.part(FILL[5])
                    settle()
                for half in range(2):
                    b = bank_of(s, WO0 + half)
                    xh = xs[:, t, half * BANK:(half + 1) * BANK]
                    dve.wait_ge(proj_ready.sem, proj_ready.at(s, WO0 + half))
                    V.tensor_tensor(xh, proj[b][:, :], xh, ALU.add).then_inc(proj_free[b], 1)
                    dve.wait_ge(proj_free[b], freed(s, WO0 + half))
                mean_square(stat[:, 0:1], xs[:, t, :], hrow[:, :], D).then_inc(mean_ready.sem, 1)
                if t == 0:
                    dve.wait_ge(ffn_params, 32 * (l + 1))
                dots.rest()
                if s > 0:
                    dve.wait_ge(rows_used, dve_rows(s - 1, 1, 0))
                dve.wait_ge(root_ready.sem, root_ready.at(s, 3))
                link(V.reciprocal(stat[:, 8:9], stat[:, 4:5]))
                V.scalar_tensor_tensor(out=h2row[:, :], in0=xs[:, t, :], scalar=stat[:, 8:9], in1=gffn[:, :],
                                       op0=ALU.mult, op1=ALU.mult).then_inc(h2_ready.sem, 1)
                if s == 0:
                    first_norm(1)
                if s > 0:
                    coefficients(s - 1)
                adds.part(PE_HEADS[0] * TOPK)
                for buf in range(2):
                    route(s, buf)
                if s > 0:
                    adds.over()
                    adds.heads(HEADS - 1 - PE_HEADS[-1] - LAST_HEADS)
                    adds.pe_sum()
                    adds.rest()

            def route(s, buf):
                n = HEADS // 2
                first = n * buf
                picks = slice(first * TOPK, (first + n) * TOPK)
                dve.wait_ge(route_ready.sem, route_ready.at(s, buf))
                for hh in range(n):
                    lists = [(first + hh) * 2 + p for p in range(2)]
                    raws = [sc[buf][:, p * BANK + hh * KEYS:p * BANK + (hh + 1) * KEYS] for p in range(2)]
                    for j, raw in zip(lists, raws):
                        noted(V.max(tops[:, j, 0:8], raw))
                    settle()
                    for j, raw in zip(lists, raws):
                        V.max_index(topi[:, j, 0:8], tops[:, j, 0:8], raw)
                        noted(V.match_replace(scores[:, j, :], tops[:, j, 0:8], raw, NEG))
                    settle()
                    for j in lists:
                        noted(V.max(tops[:, j, 8:16], scores[:, j, :]))
                    settle()
                    for j in lists:
                        noted(V.max_index(topi[:, j, 8:16], tops[:, j, 8:16], scores[:, j, :]))
                settle()
                lists = slice(2 * first, 2 * (first + n))
                noted(V.tensor_copy(topf[:, lists, :], topi[:, lists, :]))
                pairs = tops[:, lists, :].rearrange("p (h two) a -> p h two a", two=2)
                sums = cand[:, first * 256:(first + n) * 256]
                c4 = sums.rearrange("p (h a b) -> p h a b", h=n, a=TOPK)
                full = [P, n, TOPK, TOPK]
                link(V.tensor_tensor(c4, pairs[:, :, 0, :].unsqueeze(3).to_broadcast(full),
                                     pairs[:, :, 1, :].unsqueeze(2).to_broadcast(full), ALU.add))
                for h0 in range(first, first + n, 2):
                    two = [(h, cand[:, h * 256:(h + 1) * 256]) for h in (h0, h0 + 1)]
                    for h, c in two:
                        noted(V.max(best[:, h, 0:8], c))
                    settle()
                    for h, c in two:
                        noted(V.max_index(bestpos[:, h, 0:8], best[:, h, 0:8], c))
                    settle()
                    for h, c in two:
                        noted(V.match_replace(c, best[:, h, 0:8], c, NEG))
                    settle()
                    for h, c in two:
                        noted(V.max(best[:, h, 8:16], c))
                    settle()
                    for h, c in two:
                        noted(V.max_index(bestpos[:, h, 8:16], best[:, h, 8:16], c))
                settle()
                heads = slice(first, first + n)
                pw = pickw[:, s % 2, picks].rearrange("p (h k) -> p h k", h=n)
                less = V.tensor_tensor(pw, best[:, heads, :], best[:, heads, 0:1].to_broadcast([P, n, TOPK]),
                                       ALU.subtract)
                if buf == 1:
                    less.then_inc(best_ready.sem, 1)
                flatpos = bestpos[:, heads, :].rearrange("p h k -> p (h k)")
                noted(V.tensor_scalar(pos[:, 0, picks], flatpos, 4, None, ALU.logical_shift_right))
                noted(V.tensor_scalar(pos[:, 1, picks], flatpos, TOPK - 1, None, ALU.bitwise_and))
                settle()
                link(V.tensor_copy(posf[:, :, picks], pos[:, :, picks]))
                index_pairs = topf[:, lists, :].rearrange("p (h two) a -> p h two a", two=2)
                wide = [P, n * TOPK, TOPK]
                c3 = sums.rearrange("p (k a) -> p k a", a=TOPK)
                for half in range(2):
                    link(V.tensor_tensor(c3, posf[:, half, picks].unsqueeze(2).to_broadcast(wide),
                                         iota[:, :].unsqueeze(1).to_broadcast(wide), ALU.is_equal))
                    link(V.tensor_tensor(c4, c4, index_pairs[:, :, half, :].unsqueeze(2).to_broadcast(full), ALU.mult))
                    link(V.tensor_reduce(part[:, half, picks], c3, AX.X, ALU.add))
                base = float(s // TILES * EXPERTS)
                link(V.tensor_scalar(part[:, 0, picks], part[:, 0, picks], float(KEYS), base, ALU.mult, ALU.add))
                V.tensor_tensor(index[:, s % 2, picks], part[:, 0, picks], part[:, 1, picks], ALU.add)\
                    .then_inc(index_ready.sem, 1)

            def picks_softmax(s):
                pw = pickw[:, s % 2, :].rearrange("p (h k) -> p h k", h=HEADS)
                dve.wait_ge(bexp_ready.sem, bexp_ready.at(s))
                link(V.tensor_reduce(gsum[:, 0, :], pw, AX.X, ALU.add))
                link(V.reciprocal(gsum[:, 1, :], gsum[:, 0, :]))
                link(V.tensor_tensor(pw, pw, gsum[:, 1, :].unsqueeze(2).to_broadcast([P, HEADS, TOPK]), ALU.mult))

            def final_norm(t):
                dst = (hrow if t == 0 else h2row)[:, :]
                mean_square(stat[:, 0:1], xs[:, t, :], dst, D).then_inc(fin_mean, 1)
                if t == 0:
                    dve.wait_ge(gmix_in, 16 * (DEPTH + 1))
                dve.wait_ge(fin_root, t + 1)
                link(V.reciprocal(stat[:, 8:9], stat[:, 4:5]))
                V.scalar_tensor_tensor(out=dst, in0=xs[:, t, :], scalar=stat[:, 8:9], in1=gmix[:, :],
                                       op0=ALU.mult, op1=ALU.mult).then_inc(fin_row, 1)

            V.memset(headrow[:, :], 0.0).then_inc(headrow_zero, 1)
            V.memset(eps[:, :], EPS).then_inc(eps_set, 1)
            dense_first(0, Nothing())
            dense_second(0, Nothing(), Nothing())
            for s in range(1, STAGES):
                dots, adds = Retrieval(s - 1, 0), Retrieval(s - 1, 1)
                dense_first(s, dots)
                dense_second(s, dots, adds)
            picks_softmax(STAGES - 1)
            dve.wait_ge(rows_used, dve_rows(STAGES - 1, 0, 0))
            final_norm(0)
            dots = Retrieval(STAGES - 1, 0)
            dots.heads(HEADS)
            coefficients(STAGES - 1)
            adds = Retrieval(STAGES - 1, 1)
            adds.heads(PE_HEADS[0])
            adds.over()
            adds.heads(HEADS - 1 - PE_HEADS[-1] - LAST_HEADS)
            adds.pe_sum()
            adds.rest()
            dve.wait_ge(rows_used, dve_rows(STAGES, 0, 0))
            final_norm(1)

        @block.tensor
        def _(pe):
            def begin(s, use):
                b = bank_of(s, use)
                n = freed(s, use) - 1
                if n > 0:
                    pe.wait_ge(proj_free[b], n)
                return proj[b]

            def end(last):
                last.then_inc(proj_ready.sem, 1)

            def evacuated(s, use):
                pe.wait_ge(proj_free[bank_of(s, use)], freed(s, use))

            def w_arrived(s, name):
                n = s * NW + W_AT[name]
                pe.wait_ge(w_in_sem[W_SLOT[n]], 16 * W_FILLS[n])

            def transposes(s, use, sources, rows_out=P):
                bank = begin(s, use)
                for j, src in enumerate(sources):
                    last = nc.tensor.transpose(bank[0:rows_out, j * P:(j + 1) * P], src, ident[:, :])
                end(last)

            def product(s, use, lhs, rhs, width):
                bank = begin(s, use)
                kc = len(lhs)
                for c in range(kc):
                    last = nc.tensor.matmul(bank[:, 0:width], lhs[c], rhs[c], start=(c == 0), stop=(c == kc - 1))
                end(last)

            def row_chunk(s, use, name, width):
                w_arrived(s, name)
                w = w_slot(s, name, KC, width)
                product(s, use, [hT[:, c, :] for c in range(KC)], [w[:, c, :] for c in range(KC)], width)

            def turned(s, rows_use, use, b, blocks):
                evacuated(s, rows_use)
                transposes(s, use, [rowtmp[:, b, j * P:(j + 1) * P] for j in range(blocks)])

            def gate_half(s, i):
                g, second = divmod(i, 2)
                g += 2
                if not second:
                    w_arrived(s, ("gate", g))
                    begin(s, GATES[g])
                w = w_slot(s, ("gate", g), KC, BANK)
                for c in range(4 * second, 4 * second + 4):
                    last = nc.tensor.matmul(proj[bank_of(s, GATES[g])][:, :], hT[:, c, :], w[:, c, :],
                                            start=(c == 0), stop=(c == KC - 1))
                if second:
                    end(last)

            def dense_first(s):
                t = s % TILES
                nk = (t + 1) * P
                nb = t + 1
                pe.wait_ge(h_ready.sem, h_ready.at(s))
                for i in range(2):
                    transposes(s, HT0 + i, [hrow[:, c * P:(c + 1) * P] for c in range(4 * i, 4 * i + 4)])
                for i in range(2):
                    evacuated(s, HT0 + i)
                row_chunk(s, PC, "c", C_WIDTH)
                if s == 0:
                    pe.wait_ge(head_in, 48)
                    nc.tensor.matmul(psO[0:BIAS_HEADS + 1, :], headrow[:, :], onehot, start=True, stop=True)\
                        .then_inc(table_ps, 1)
                row_chunk(s, AQR, "aq", A_HEADS * HD)
                row_chunk(s, AKR, "ak", A_HEADS * HD)
                turned(s, AQR, AQT, 0, 3)
                row_chunk(s, AV, "av", A_HEADS * HD)
                turned(s, AKR, AKT, 1, 3)
                row_chunk(s, BQR, "bq", BANK)
                row_chunk(s, BKR, "bk", BANK)
                turned(s, BQR, BQT, 0, 4)
                row_chunk(s, BV, "bv", B_HEADS * P)
                turned(s, BKR, BKT, 1, 4)
                pe.wait_ge(cnorm_ready.sem, cnorm_ready.at(s))
                transposes(s, CT, [cnorm[:, j * P:(j + 1) * P] for j in range(3)])
                row_chunk(s, G0, ("gate", 0), BANK)
                evacuated(s, CT)
                for i in range(2):
                    n = 3 * C_QK
                    product(s, CQ0 + i, [cT[:, c, :] for c in range(2)],
                            [wuq[:, c, i * n:(i + 1) * n] for c in range(2)], n)
                for i in range(2):
                    n = 3 * P
                    product(s, CKV0 + i, [cT[:, 2, :]], [wukv[:, i * n:(i + 1) * n]], n)
                row_chunk(s, G1, ("gate", 1), BANK)
                pe.wait_ge(qrope_ready.sem, qrope_ready.at(s))
                for i, (h0, h1) in enumerate(((0, 4), (4, 6))):
                    transposes(s, CQT0 + i, [qrow[:, h, :] for h in range(h0, h1)], C_QK)
                pe.wait_ge(krope_ready.sem, krope_ready.at(s))
                for i in range(2):
                    evacuated(s, CKV0 + i)
                for i, (h0, h1) in enumerate(((0, 4), (4, 6))):
                    transposes(s, CKT0 + i, [krow[:, h, :] for h in range(h0, h1)], C_QK)

                for i in range(GROUPS + 2):
                    if i < GROUPS:
                        score(s, i, nk)
                    if i in GATE_HALVES:
                        gate_half(s, GATE_HALVES.index(i))
                    if 0 <= i - 1 < GROUPS:
                        transpose_probs(s, i - 1, nb)
                    if 0 <= i - 2 < GROUPS:
                        times_v(s, i - 2, nb)

            def score(s, g, nk):
                b, (kind, j) = g % 2, kind_of(g)
                if g == 0:
                    evacuated(s, AKT)
                if g == 3:
                    evacuated(s, BKT)
                if g == 7:
                    evacuated(s, CKT0)
                    evacuated(s, CKT1)
                if g >= 2:
                    pe.wait_ge(neg_ready.sem, neg_ready.at(s, g - 2))
                elif s > 0:
                    pe.wait_ge(index_ready.sem, index_ready.at(s - 1, 1))
                for m in range(2):
                    half = slice(m * HD, (m + 1) * HD)
                    if kind == "A":
                        q, k = qTA[half, j, :], kTA[half, j, 0:nk]
                    elif kind == "B":
                        q, k = qTB[half, j, :], kTB[half, j, 0:nk]
                    else:
                        q, k = qTC[:, 2 * j + m, :], kTC[:, 2 * j + m, 0:nk]
                    last = nc.tensor.matmul(sc[b][:, m * BANK:m * BANK + nk], q, k, start=True, stop=True)
                last.then_inc(s_ready.sem, 1)

            def transpose_probs(s, g, nb):
                b = g % 2
                maps = 1 if kind_of(g)[0] == "B" else 2
                pe.wait_ge(p_ready.sem, p_ready.at(s, g))
                if g == 0 and s > 1:
                    pe.wait_ge(pe_sum_used, 2 * (s - 1))
                if g > 0 or s > 0:
                    pe.wait_ge(pTs_ready.sem, pTs_ready.at(s, g - 1))
                for m in range(maps):
                    for c in range(nb):
                        at = (m * nb + c) * P
                        last = nc.tensor.transpose(psT[:, at:at + P], probs[:, b, m, c * P:(c + 1) * P], ident[:, :])
                last.then_inc(pT_ready.sem, 1)

            def times_v(s, g, nb):
                b, (kind, j) = g % 2, kind_of(g)
                pe.wait_ge(pTs_ready.sem, pTs_ready.at(s, g))
                if g > 0 or s > 0:
                    pe.wait_ge(o_used.sem, o_used.at(s, g - 1))
                else:
                    pe.wait_ge(table_sb, 1)
                for m in range(1 if kind == "B" else 2):
                    width = 2 * HD if kind == "B" else HD
                    for c in range(nb):
                        v = {"A": vA, "B": vB, "C": vC}[kind][:, c, (j if kind == "B" else 2 * j + m) * width:][:, 0:width]
                        at = (m * nb + c) * P
                        last = nc.tensor.matmul(psO[:, m * HD:m * HD + width], probsT[:, b, at:at + P], v,
                                                start=(c == 0), stop=(c == nb - 1))
                last.then_inc(o_ready.sem, 1)

            def dense_second(s):
                pe.wait_ge(y_ready.sem, y_ready.at(s))
                for i, (b0, b1) in enumerate(((0, 4), (4, 8), (8, 10))):
                    transposes(s, YT0 + i, [y[:, b * P:(b + 1) * P] for b in range(b0, b1)])
                for i in range(3):
                    evacuated(s, YT0 + i)
                branches = (("wa", 0, 3), ("wb", 3, 4), ("wc", 7, 3))
                for br, (name, b0, kc) in enumerate(branches):
                    w_arrived(s, name)
                    w = w_slot(s, name, kc, D)
                    for half in range(2):
                        product(s, BR0 + 2 * br + half, [yT[:, b0 + c, :] for c in range(kc)],
                                [w[:, c, half * BANK:(half + 1) * BANK] for c in range(kc)], BANK)
                for i in range(2):
                    pe.wait_ge(mix_ready.sem, mix_ready.at(s, i))
                    transposes(s, MT0 + i, [mix[:, c * P:(c + 1) * P] for c in range(4 * i, 4 * i + 4)])
                for i in range(2):
                    evacuated(s, MT0 + i)
                for i in range(2):
                    row_chunk(s, WO0 + i, ("wo", i), BANK)
                pe.wait_ge(h2_ready.sem, h2_ready.at(s))
                for i in range(2):
                    transposes(s, H2T0 + i, [h2row[:, c * P:(c + 1) * P] for c in range(4 * i, 4 * i + 4)])
                for i in range(2):
                    evacuated(s, H2T0 + i)
                for i in range(2):
                    row_chunk(s, PQR0 + i, ("pq", i), BANK)
                for i in range(2):
                    turned(s, PQR0 + i, PQT0 + i, i, 4)
                for buf in range(2):
                    evacuated(s, PQT0 + buf)
                    for hh in range(4):
                        h = 4 * buf + hh
                        for p in range(2):
                            half = slice(p * HD, (p + 1) * HD)
                            at = p * BANK + hh * KEYS
                            last = nc.tensor.matmul(sc[buf][:, at:at + KEYS], pqT[half, h, :], keys[half, h, :],
                                                    start=True, stop=True)
                    last.then_inc(route_ready.sem, 1)

            def add_rows(s):
                for j in range(PE_PICKS):
                    slot = j % RING
                    pe.wait_ge(row_in[slot], (row_step(s, 1, PE_HEADS[0] * TOPK + j) // RING + 1) * 16)
                    pe.wait_ge(diag_ready, s * PE_PICKS + j + 1)
                    for half in range(2):
                        last = nc.tensor.matmul(vsum[half][:, :], diags[:, j % DIAGS, :],
                                                rows[:, slot, half * BANK:(half + 1) * BANK],
                                                start=(j == 0), stop=(j == PE_PICKS - 1))
                    last.then_inc(pe_rows_used, 1)

            pe.wait_ge(ident_sem, 16)
            for s in range(STAGES):
                dense_first(s)
                dense_second(s)
                if s > 0:
                    add_rows(s - 1)
            pe.wait_ge(pe_sum_used, 2 * (STAGES - 1))
            add_rows(STAGES - 1)


def shape_constants():
    import numpy as np
    ident = np.eye(P, dtype=np.float32)
    dist = SEQ - 1 - np.arange(BANK)
    exact = BUCKETS // 2
    nf = np.maximum(dist, exact).astype(np.float32)
    large = exact + (np.log(nf / np.float32(exact)) / np.float32(math.log(MAX_DISTANCE / exact))
                     * np.float32(BUCKETS - exact)).astype(np.int32)
    bucket = np.where(np.maximum(dist, 0) < exact, np.maximum(dist, 0), np.minimum(large, BUCKETS - 1))
    occurs = lambda d: sum((d >= 0) & (d <= window) & (d % dilation == 0) for window, dilation in A_CONFIGS)
    onehot = np.zeros((BUCKETS + 2, BANK), np.float32)
    onehot[bucket, np.arange(BANK)] = dist >= 0
    onehot[BUCKETS] = np.where(dist >= 0, 0.0, NEG)
    onehot[BUCKETS + 1] = np.where((dist >= 0) & (occurs(dist) == 0), NEG, 0.0)
    maskrow = np.ones((2, BIAS_HEADS + 1), np.float32)
    maskrow[1, A_HEADS:] = 0.0
    count = occurs(P + np.arange(P)[:, None] - np.arange(SEQ)[None, :]).astype(np.float32)
    half = ROPE // 2
    inv = np.float32(10000.0) ** (-np.arange(half, dtype=np.float32) / np.float32(half))
    ang = np.arange(SEQ, dtype=np.float32)[:, None] * inv[None, :]
    rope = np.stack([np.tile(np.cos(ang), 7), np.tile(np.sin(ang), 7)], 1).astype(np.float32)
    iota = np.tile(np.arange(TOPK, dtype=np.float32), (P, 1))
    return ident, onehot, maskrow, count, rope, iota


def kernel(**inputs):
    import numpy as np
    import concourse.bacc as bacc
    from concourse.bass_utils import run_bass_kernel_spmd

    a = {k: np.asarray(v) for k, v in inputs.items()}
    ident, onehot, maskrow, count, rope, iota = shape_constants()
    laid = {
        "x": a["x"].reshape(TILES, P, D), "rel_bias": a["rel_bias"], "w_in": a["w_in"], "g_mix": a["g_mix"],
        "w_uq": a["w_uq"], "g_cq": a["g_cq"], "w_ukv": a["w_ukv"], "g_ckv": a["g_ckv"],
        "lam_vecs": np.stack([a["lam_q1"], a["lam_k1"], a["lam_q2"], a["lam_k2"]], 1).reshape(-1),
        "g_subln": a["g_subln"], "w_a": a["w_branch_a"], "w_b": a["w_branch_b"], "w_c": a["w_branch_c"],
        "w_out": a["w_out"], "g_ffn": a["g_ffn"], "w_pq": a["w_peer_q"],
        "keysT": a["peer_sub_keys"].transpose(0, 2, 4, 1, 3).reshape(DEPTH, P, HEADS * KEYS),
        "peer_u": a["peer_u"].reshape(DEPTH * EXPERTS, D), "peer_v": a["peer_v"].reshape(DEPTH * EXPERTS, D),
        "g_final": a["g_final"], "ident_in": ident, "onehot_in": onehot, "maskrow_in": maskrow, "count_in": count,
        "rope_in": rope, "iota_in": iota,
    }
    nc = bacc.Bacc("TRN2", target_bir_lowering=False, num_devices=1)
    arrays, args = {}, []
    for name, v in laid.items():
        v = np.ascontiguousarray(v)
        arrays[name] = v
        args.append(nc.dram_tensor(name, list(v.shape), mybir.dt.from_np(v.dtype), kind="ExternalInput").ap())
    args.append(nc.dram_tensor("out", [TILES, P, D], F32, kind="ExternalOutput").ap())
    trunk(nc, *args)
    r = run_bass_kernel_spmd(nc, [arrays], core_ids=[0])
    return r.results[0]["out"].reshape(1, SEQ, D)
```
